# Optimizing a Trainium2 kernel written in Bass

```python
import math
import jax, jax.numpy as jnp
from jax import lax
import numpy as np

D_MODEL = 2048
BATCH = 1
SEQ = 256
DEPTH = 1

N_MEM = 256
MIX_WIDTH = D_MODEL
ATTN_WIDTH = MIX_WIDTH // 2
HG_WIDTH = MIX_WIDTH - ATTN_WIDTH
ATTN_HEAD_DIM = 128
ATTN_HEADS = ATTN_WIDTH // ATTN_HEAD_DIM
HG_EXPAND = 128
HG_HEADS = HG_WIDTH // HG_EXPAND
HG_VDIM = HG_WIDTH // HG_HEADS
HG_CHUNK = 64
DILATED_BRANCHES = ((128, 1), (512, 4), (2048, 16))
Q_BLOCK = 128
REL_BUCKETS = 32
REL_MAX_DIST = 2048
CROSS_HEADS = 4
CROSS_HEAD_DIM = D_MODEL // CROSS_HEADS
D_FF = ((8 * D_MODEL + 3 * 256 - 1) // (3 * 256)) * 256
IN_SIZES = (ATTN_WIDTH, ATTN_WIDTH, ATTN_WIDTH, HG_WIDTH, HG_WIDTH, HG_WIDTH, HG_WIDTH)
IN_COLS = sum(IN_SIZES)
N_NORMS = 7
RMS_EPS = 1e-6
NEG_INF = -1e30

kernel_name = "hybrid_dilated_attn_hgrn2_trunk"

def rmsnorm(x, g):
    xf = x.astype(jnp.float32)
    y = xf * lax.rsqrt(jnp.mean(xf * xf, axis=-1, keepdims=True) + RMS_EPS)
    return (y * g.astype(jnp.float32)).astype(x.dtype)

def rel_bucket(dist):
    max_exact = REL_BUCKETS // 2
    d_f = jnp.maximum(dist, 1).astype(jnp.float32)
    large = max_exact + (jnp.log(d_f / max_exact) / math.log(REL_MAX_DIST / max_exact)
                         * (REL_BUCKETS - max_exact)).astype(jnp.int32)
    large = jnp.minimum(large, REL_BUCKETS - 1)
    return jnp.where(dist < max_exact, dist, large)

def dilated_branch(q, k, v, rel_bias, window, dilation):
    B, S, H, Dh = q.shape
    band = window // dilation
    assert band <= Q_BLOCK
    M = S // dilation
    Mp = -(-M // Q_BLOCK) * Q_BLOCK
    nb = Mp // Q_BLOCK

    def split(t):
        t = t.reshape(B, M, dilation, H, Dh)
        return jnp.pad(t, ((0, 0), (0, Mp - M), (0, 0), (0, 0), (0, 0)))

    def kwin(t):
        tp = jnp.pad(split(t), ((0, 0), (Q_BLOCK, 0), (0, 0), (0, 0), (0, 0)))
        tp = tp.reshape(B, nb + 1, Q_BLOCK, dilation, H, Dh)
        return jnp.concatenate([tp[:, :-1], tp[:, 1:]], axis=2)

    qs = split(q).reshape(B, nb, Q_BLOCK, dilation, H, Dh)
    ks, vs = kwin(k), kwin(v)
    scores = jnp.einsum('bnqrhd,bnkrhd->bnrhqk', qs, ks).astype(jnp.float32) * (Dh ** -0.5)

    qi = jnp.arange(Q_BLOCK)[:, None]
    kj = jnp.arange(2 * Q_BLOCK)[None, :]
    m = qi - kj + Q_BLOCK
    bucket = rel_bucket(jnp.maximum(m, 0) * dilation)
    bias = jnp.transpose(rel_bias[bucket].astype(jnp.float32), (2, 0, 1))
    band_ok = (m >= 0) & (m <= band)
    blk = jnp.arange(nb)[:, None, None]
    start_ok = (blk * Q_BLOCK + kj[None] - Q_BLOCK) >= 0
    valid = band_ok[None] & start_ok
    logits = jnp.where(valid[None, :, None, None], scores + bias, NEG_INF)
    lse = jax.nn.logsumexp(logits, axis=-1)
    p = jnp.exp(logits - lse[..., None])
    o = jnp.einsum('bnrhqk,bnkrhd->bnqrhd', p.astype(vs.dtype), vs)
    o = o.reshape(B, Mp, dilation, H, Dh)[:, :M].reshape(B, S, H, Dh)
    lse = jnp.transpose(lse, (0, 1, 4, 2, 3)).reshape(B, Mp, dilation, H)[:, :M].reshape(B, S, H)
    return o, lse

def dilated_attention(q, k, v, rel_bias):
    outs, lses = [], []
    for window, dilation in DILATED_BRANCHES:
        o, l = dilated_branch(q, k, v, rel_bias, window, dilation)
        outs.append(o)
        lses.append(l)
    w = jax.nn.softmax(jnp.stack(lses), axis=0)
    o = jnp.einsum('gbsh,gbshd->bshd', w.astype(q.dtype), jnp.stack(outs))
    return o

def hgrn2(fz, iv, qz, gz, lb, hg_gain):
    B, S, _ = fz.shape
    nc = S // HG_CHUNK
    f = lb + (1.0 - lb) * jax.nn.sigmoid(fz.astype(jnp.float32))
    log_f = jnp.log(f)
    kk = 1.0 - f
    qq = jax.nn.silu(qz.astype(jnp.float32))
    vv = iv.astype(jnp.float32)

    def chunks(t, dim):
        return jnp.transpose(t.reshape(B, nc, HG_CHUNK, HG_HEADS, dim), (1, 0, 3, 2, 4))

    xs = (chunks(qq, HG_EXPAND), chunks(kk, HG_EXPAND), chunks(vv, HG_VDIM), chunks(log_f, HG_EXPAND))
    tri = jnp.tril(jnp.ones((HG_CHUNK, HG_CHUNK), dtype=bool))

    def step(state, inp):
        qc, kc, vc, lfc = inp
        b = jnp.cumsum(lfc, axis=-2)
        o_inter = jnp.einsum('bhck,bhkv->bhcv', qc * jnp.exp(b), state)
        diff = b[:, :, :, None, :] - b[:, :, None, :, :]
        decay = jnp.exp(jnp.where(tri[:, :, None], diff, -jnp.inf))
        A = jnp.einsum('bhtk,bhtsk,bhsk->bhts', qc, decay, kc)
        o = o_inter + jnp.einsum('bhts,bhsv->bhtv', A, vc)
        b_last = b[:, :, -1:, :]
        new_state = jnp.exp(b_last[:, :, 0, :])[..., None] * state + \
            jnp.einsum('bhsk,bhsv->bhkv', kc * jnp.exp(b_last - b), vc)
        return new_state, o

    s0 = jnp.zeros((B, HG_HEADS, HG_EXPAND, HG_VDIM), jnp.float32)
    _, o = lax.scan(step, s0, xs)
    o = jnp.transpose(o, (1, 0, 3, 2, 4)).reshape(B, S, HG_HEADS, HG_VDIM)
    o = o * lax.rsqrt(jnp.mean(o * o, axis=-1, keepdims=True) + RMS_EPS)
    o = o * hg_gain.astype(jnp.float32).reshape(HG_HEADS, HG_VDIM)
    o = o.reshape(B, S, HG_WIDTH) * jax.nn.silu(gz.astype(jnp.float32))
    return o.astype(fz.dtype)

def setup_inputs(seed: int = 0) -> dict:
    key = jax.random.key(seed)
    ks = jax.random.split(key, 14)
    f32 = jnp.float32
    nrm = lambda k, shape, scale: jax.random.normal(k, shape, f32) * scale
    return {
        "x": nrm(ks[0], (BATCH, SEQ, D_MODEL), 1.0),
        "mem": nrm(ks[1], (BATCH, N_MEM, D_MODEL), 1.0),
        "rel_bias": nrm(ks[2], (REL_BUCKETS, ATTN_HEADS), 0.5),
        "lb_logits": nrm(ks[3], (DEPTH, HG_WIDTH), 0.5),
        "norm_gains": 1.0 + nrm(ks[4], (DEPTH, N_NORMS, D_MODEL), 0.1),
        "w_in": nrm(ks[5], (DEPTH, D_MODEL, IN_COLS), D_MODEL ** -0.5),
        "hg_norm": 1.0 + nrm(ks[6], (DEPTH, HG_WIDTH), 0.1),
        "w_out": nrm(ks[7], (DEPTH, MIX_WIDTH, D_MODEL), MIX_WIDTH ** -0.5),
        "w_cq": nrm(ks[8], (DEPTH, D_MODEL, D_MODEL), D_MODEL ** -0.5),
        "w_ckv": nrm(ks[9], (DEPTH, D_MODEL, 2 * D_MODEL), D_MODEL ** -0.5),
        "w_co": nrm(ks[10], (DEPTH, D_MODEL, D_MODEL), D_MODEL ** -0.5),
        "w_gate_up": nrm(ks[11], (DEPTH, D_MODEL, 2 * D_FF), D_MODEL ** -0.5),
        "w_down": nrm(ks[12], (DEPTH, D_FF, D_MODEL), D_FF ** -0.5),
    }

def reference(x, mem, rel_bias, lb_logits, norm_gains, w_in, hg_norm, w_out,
              w_cq, w_ckv, w_co, w_gate_up, w_down):
    B, S, D = x.shape
    n_mem = mem.shape[1]
    P = jax.nn.softmax(lb_logits.astype(jnp.float32), axis=0)
    lb_all = jnp.cumsum(P, axis=0) - P
    split_idx = [int(i) for i in np.cumsum(IN_SIZES)[:-1]]

    for l in range(DEPTH):
        g = norm_gains[l]
        h = rmsnorm(x, g[0])
        proj = h @ w_in[l]
        aq, ak, av, fz, iv, qz, gz = jnp.split(proj, split_idx, axis=-1)
        shp = (B, S, ATTN_HEADS, ATTN_HEAD_DIM)
        attn = dilated_attention(aq.reshape(shp), ak.reshape(shp), av.reshape(shp), rel_bias)
        attn = attn.reshape(B, S, ATTN_WIDTH)
        hg = hgrn2(fz, iv, qz, gz, lb_all[l], hg_norm[l])
        mix = jnp.concatenate([attn, hg], axis=-1) @ w_out[l]
        x = x + rmsnorm(mix, g[1])
        hc = rmsnorm(x, g[2])
        mn = rmsnorm(mem, g[3])
        cq = (hc @ w_cq[l]).reshape(B, S, CROSS_HEADS, CROSS_HEAD_DIM)
        ck, cv = jnp.split(mn @ w_ckv[l], 2, axis=-1)
        ck = ck.reshape(B, n_mem, CROSS_HEADS, CROSS_HEAD_DIM)
        cv = cv.reshape(B, n_mem, CROSS_HEADS, CROSS_HEAD_DIM)
        s = jnp.einsum('bshd,bmhd->bhsm', cq, ck).astype(jnp.float32) * (CROSS_HEAD_DIM ** -0.5)
        p = jax.nn.softmax(s, axis=-1).astype(cv.dtype)
        co = jnp.einsum('bhsm,bmhd->bshd', p, cv).reshape(B, S, D) @ w_co[l]
        x = x + rmsnorm(co, g[4])
        hf = rmsnorm(x, g[5])
        gate, up = jnp.split(hf @ w_gate_up[l], 2, axis=-1)
        y = (jax.nn.silu(gate) * up) @ w_down[l]
        x = x + rmsnorm(y, g[6])
    return x


_drawn_inputs = setup_inputs


def setup_inputs(seed=0):
    import zlib

    import numpy as np

    out = dict(_drawn_inputs(seed))
    spreads = {}
    factors = {}
    for name, (base, spread) in spreads.items():
        noise = np.random.default_rng([zlib.crc32(name.encode()), seed]).standard_normal(out[name].shape)
        drawn = base * np.exp(spread * noise) if base else spread * noise
        out[name] = __import__('jax').numpy.asarray(drawn.astype(out[name].dtype))
    for name, factor in factors.items():
        out[name] = (out[name] * factor).astype(out[name].dtype)
    return out
```

```python
import math
from contextlib import ExitStack

import numpy as np

import concourse.bass as bass
from concourse import mybir

F32 = mybir.dt.float32
F32R = mybir.dt.float32r
BF16 = mybir.dt.bfloat16
U8 = mybir.dt.uint8
I32 = mybir.dt.int32
ALU = mybir.AluOpType
ACT = mybir.ActivationFunctionType
AX = mybir.AxisListType

P = 128
D = 2048
SEQ = 256
TT = SEQ // P
DC = D // P
HEADS = 8
DH = 128
CROSS_HEADS = 4
CROSS_DH = D // CROSS_HEADS
CC = CROSS_DH // P
D_FF = 5632
NT = 512
NB = 384
F_TILES = D_FF // NT
F_CHUNKS = NT // P
GROUP_TILES = (4, 4, 3)
REL_BUCKETS = 32
REL_MAX_DIST = 2048
BRANCHES = ((128, 1), (512, 4), (2048, 16))
EPS = 1e-6
MASKED = -1e30
LEVELS = 7
BETA = 384
RING = 4
JOB_G = DC // 2
BODY_G = 3 * JOB_G
G_BODY = 2 * JOB_G
G_LAST_HEAD = G_BODY + (HEADS - 1) * BODY_G
G_OUT = G_LAST_HEAD + JOB_G
G_CQ = G_OUT + 4 * JOB_G
G_CO = G_CQ + 4 * JOB_G
G_FFN = G_CO + 4 * JOB_G
DMA = 16


def layer_kernel(nc, x, xt, mem, memt, rel_bias, ident_in, flip_in, masks_in, onehot_in, gain_cols_in,
                 gain_rows_in, hg_gain_in, w_in_a, w_in_b, w_ckv, w_out, w_cq, w_co, w_gate_up,
                 w_down, beta_dram, out):
    ctx = ExitStack()
    with ctx:
        def sb(name, shape, dt=F32):
            return ctx.enter_context(nc.sbuf_tensor(name, shape, dt))

        def psum(name):
            return ctx.enter_context(nc.psum_tensor(name, [P, 512], F32))

        def sem(name):
            return ctx.enter_context(nc.semaphore(name))

        raw = sb("raw", [P, RING, 2 * NT])
        w_hi = sb("w_hi", [P, RING, 2 * NT], F32R)
        w_lo = sb("w_lo", [P, RING, 2 * NT], F32R)
        a_hi = sb("a_hi", [P, DC, SEQ], F32R)
        a_lo = sb("a_lo", [P, DC, SEQ], F32R)
        b_hi = sb("b_hi", [P, DC, SEQ], F32R)
        b_lo = sb("b_lo", [P, DC, SEQ], F32R)
        r1 = sb("r1", [P, 2 * D])
        r2 = sb("r2", [P, 2 * D])
        r3 = sb("r3", [P, 4 * D])
        r4 = sb("r4", [P, D])
        work = sb("work", [P, 4096])
        ident = sb("ident", [P, P])
        ones = sb("ones", [P, P])
        masks = sb("masks", [P, LEVELS, P], U8)
        gcol = sb("gcol", [P, 4, DC])
        hg_gain = sb("hg_gain", [P, HEADS])
        eps_col = sb("eps_col", [P, 1])[:, :]
        junk = sb("junk", [P, 4, NT], BF16)
        stat = sb("stat", [P, 64])

        x_nat = r1[:, :].rearrange("p (t d) -> p t d", t=TT)
        mix_t = r1[:, :].rearrange("p (c s) -> p c s", c=DC)
        sub = r1[:, :].rearrange("p (t d) -> p t d", t=TT)
        mem_nat = r2[:, :].rearrange("p (t d) -> p t d", t=TT)
        res = r2[:, :].rearrange("p (t d) -> p t d", t=TT)
        decay = r2[:, 0:2048].rearrange("p (l s) -> p l s", l=LEVELS + 1)
        proj_a = r2[:, 2048:3072].rearrange("p (t n) -> p t n", t=TT)
        proj_b = r2[:, 3072:3840].rearrange("p (t n) -> p t n", t=TT)
        x_t = r3[:, 0:4096].rearrange("p (c s) -> p c s", c=DC)
        mem_t = r3[:, 4096:8192].rearrange("p (c s) -> p c s", c=DC)
        ckv = r3[:, :].rearrange("p (t n) -> p t n", t=TT)
        gs = r3[:, 1024:2048].rearrange("p (t n) -> p t n", t=TT)
        hid = r3[:, 2048:3072].rearrange("p (t n) -> p t n", t=TT)
        yg = r3[:, 4096:8192].rearrange("p (t d) -> p t d", t=TT)
        bias_rev = r1[:, 0:HEADS * SEQ].rearrange("p (h j) -> p h j", h=HEADS)
        bias = r4[:, :].rearrange("p (h j) -> p h j", h=HEADS)
        gain_row = r4
        qk_t = work[:, 0:512]
        sig = work[:, 512:1024]
        qg = work[:, 1024:1280]
        kk = work[:, 1280:1536]
        logf = work[:, 1536:1792]
        b = work[:, 1792:2048]
        att = work[:, 2048:2304]
        att_x = work[:, 2304:2432]
        prob = work[:, 2432:2816]
        prob_t = work[:, 2816:3200]
        gsil = work[:, 3200:3456].rearrange("p (t n) -> p t n", t=TT)
        y_hg = work[:, 3456:3712].rearrange("p (t n) -> p t n", t=TT)
        onehot = work[0:REL_BUCKETS + 1, 0:BETA]
        rel_sb = work[0:REL_BUCKETS + 1, BETA:BETA + HEADS]
        flip = work[:, 1024:1024 + P]
        masks_wide = work[:, 1152:1152 + LEVELS * P].bitcast(I32).rearrange("p (l n) -> p l n", l=LEVELS)
        beta_sb = work[0:HEADS, 512:512 + BETA]
        cq = work[:, 0:1024].rearrange("p (t n) -> p t n", t=TT)
        cq_t = work[:, 1024:2048].rearrange("p (c s) -> p c s", c=CC)
        ck_t = work[:, 2048:3072].rearrange("p (c s) -> p c s", c=CC)
        cprob = work[:, 3072:3584].rearrange("p (t m) -> p t m", t=TT)
        cprob_t = work[:, 3584:4096].rearrange("p (m s) -> p m s", m=TT)
        ssq = stat[:, 0:2]
        rstd_x = stat[:, 2:4]
        ssq_m = stat[:, 4:6]
        rstd_m = stat[:, 6:8]
        neg_max = stat[:, 8:10]
        row_sum = stat[:, 10:12]
        ssq_o = stat[:, 12:14]
        rstd_o = stat[:, 14:16]
        ssq_n = stat[:, 16:24].rearrange("p (t n) -> p t n", t=TT)
        rstd_n = stat[:, 24:26]
        ssq_r = stat[:, 26:34].rearrange("p (t n) -> p t n", t=TT)
        rstd_r = stat[:, 34:36]

        acc = [[psum("acc00"), psum("acc01")], [psum("acc10"), psum("acc11")]]
        s0, s1, s2, s3 = psum("s0"), psum("s1"), psum("s2"), psum("s3")
        small = [s0, s1, s2, s3]

        raw_landed = [sem(f"raw_landed{i}") for i in range(RING)]
        hi_ready, lo_ready, granule_used = sem("hi_ready"), sem("lo_ready"), sem("granule_used")
        acc_free = [sem("acc_free0"), sem("acc_free1")]
        xt_landed = [sem(f"xt_landed{i}") for i in range(JOB_G)]
        gcol_landed, rel_landed, ident_landed, const_landed = (
            sem("gcol_landed"), sem("rel_landed"), sem("ident_landed"), sem("const_landed"))
        mem_landed, x_landed, memt_landed = sem("mem_landed"), sem("x_landed"), sem("memt_landed")
        masks_ready = sem("masks_ready")
        consts_set, rel_ones_set = sem("consts_set"), sem("rel_ones_set")
        beta_done, beta_stored, bias_landed, flip_done, bias_ready = (
            sem("beta_done"), sem("beta_stored"), sem("bias_landed"), sem("flip_done"), sem("bias_ready"))
        a_hi_ready, a_lo_ready, b_hi_ready, b_lo_ready = (
            sem("a_hi_ready"), sem("a_lo_ready"), sem("b_hi_ready"), sem("b_lo_ready"))
        squares_ready, log_ready, rstd_ready = sem("squares_ready"), sem("log_ready"), sem("rstd_ready")
        qk_turned, fz_turned, qk_copied = sem("qk_turned"), sem("fz_turned"), sem("qk_copied")
        sig_ready, qg_ready, kk_ready = sem("sig_ready"), sem("qg_ready"), sem("kk_ready")
        logf_ready, b_ready, decay_log, decay_ready, factors_ready = (
            sem("logf_ready"), sem("b_ready"), sem("decay_log"), sem("decay_ready"), sem("factors_ready"))
        level_done, level_merged, cross_done, cross_copied = (
            sem("level_done"), sem("level_merged"), sem("cross_done"), sem("cross_copied"))
        o_done, o_squared, o_log, o_rstd, y_ready, y_turned = (
            sem("o_done"), sem("o_squared"), sem("o_log"), sem("o_rstd"), sem("y_ready"), sem("y_turned"))
        gz_sig, gz_silu = sem("gz_sig"), sem("gz_silu")
        scores_done, logits_ready, max_ready, prob_exp, sum_inv = (
            sem("scores_done"), sem("logits_ready"), sem("max_ready"), sem("prob_exp"), sem("sum_inv"))
        prob_ready, prob_turned, prob_t_ready, pv_done, attn_copied = (
            sem("prob_ready"), sem("prob_turned"), sem("prob_t_ready"), sem("pv_done"), sem("attn_copied"))
        s3_copied = sem("s3_copied")
        gain_landed, res_landed = sem("gain_landed"), sem("res_landed")
        sub0_scaled, sub1_squared, res_ready, res_turned, res_squared = (
            sem("sub0_scaled"), sem("sub1_squared"), sem("res_ready"), sem("res_turned"), sem("res_squared"))
        cqk_turned, cqk_t_ready, cscores_done, cmax_ready, cbias_ready, cprob_exp, csum_inv = (
            sem("cqk_turned"), sem("cqk_t_ready"), sem("cscores_done"), sem("cmax_ready"), sem("cbias_ready"),
            sem("cprob_exp"), sem("csum_inv"))
        cprob_ready, cprob_turned, cprob_t_ready, cpv_done = (
            sem("cprob_ready"), sem("cprob_turned"), sem("cprob_t_ready"), sem("cpv_done"))
        hid_turned = sem("hid_turned")
        y_squared, yg_ready, out_ready, out_stored = (
            sem("y_squared"), sem("yg_ready"), sem("out_ready"), sem("out_stored"))

        def attn_chunk(h):
            return 14 if isinstance(h, int) and h == HEADS - 1 else h

        def hg_chunk(h):
            return 15 if isinstance(h, int) and h == HEADS - 1 else h + 7

        def tail_pair(n):
            return (n + 1) % 2

        def tail_uses(n):
            return n // 2 + (HEADS if n % 2 == 0 else 2 * HEADS)

        JOB_FFN = 12

        groups, tile0, g0, j0 = [], 0, G_FFN, JOB_FFN
        for tiles in GROUP_TILES:
            groups.append((tile0, tiles, g0, j0))
            tile0 += tiles
            g0 += tiles * 2 * JOB_G + 4 * tiles * F_CHUNKS // 2
            j0 += tiles * 2 + 4
        G_END = g0

        NORM_MEM, NORM_X, NORM_OUT, NORM_CQ, NORM_CO, NORM_FFN, NORM_Y = range(1, 8)

        block = ctx.enter_context(nc.Block())

        @block.sync
        def _(sp):
            def load(g, source, width, it=0, per=0):
                if g >= RING:
                    sp.wait_ge(lo_ready, it * per + (g - RING + 1))
                sp.dma_start(raw[:, g % RING, 0:width], source).then_inc(raw_landed[g % RING], DMA)

            def load_job(g, source, width, it=0, per=0):
                for j in range(JOB_G):
                    load(g + j, source[j], width, it, per)

            xt_v = xt.rearrange("(q c p) s -> q p c s", q=JOB_G, p=P)
            for j in range(JOB_G):
                sp.dma_start(x_t[:, 2 * j:2 * j + 2, :], xt_v[j]).then_inc(xt_landed[j], DMA)
                if j == 0:
                    sp.dma_start(gcol[:, :, :], gain_cols_in).then_inc(gcol_landed, DMA)
                load(j, w_in_a[0, j], 2 * NT)
            load_job(JOB_G, w_in_b[0], 2 * NB)
            with sp.Fori(0, HEADS - 1) as h:
                for j in range(JOB_G):
                    load(G_BODY + j, w_ckv[h, j], 2 * NT, h, BODY_G)
                for j in range(JOB_G):
                    load(G_BODY + JOB_G + j, w_in_a[h + 1, j], 2 * NT, h, BODY_G)
                for j in range(JOB_G):
                    load(G_BODY + 2 * JOB_G + j, w_in_b[h + 1, j], 2 * NB, h, BODY_G)
            load_job(G_LAST_HEAD, w_ckv[HEADS - 1], 2 * NT)
            for n in range(4):
                if n == 2:
                    sp.wait_ge(y_turned, HEADS)
                    sp.wait_ge(gz_silu, HEADS)
                    sp.dma_start(res, x.rearrange("(t p) d -> p t d", p=P)).then_inc(res_landed, DMA)
                if n == 1:
                    sp.wait_ge(logits_ready, HEADS)
                    sp.dma_start(gain_row[:, :], gain_rows_in[0:1, :].to_broadcast((P, D))).then_inc(gain_landed, DMA)
                load_job(G_OUT + n * JOB_G, w_out[n], 2 * NT)
            for n in range(4):
                load_job(G_CQ + n * JOB_G, w_cq[n], 2 * NT)
            sp.wait_ge(res_ready, 8)
            sp.dma_start(gain_row[:, :], gain_rows_in[1:2, :].to_broadcast((P, D))).then_inc(gain_landed, DMA)
            for n in range(4):
                load_job(G_CO + n * JOB_G, w_co[n], 2 * NT)
            for n, (tile0, tiles, g0, _) in enumerate(groups):
                for job in range(2):
                    load_job(g0 + job * JOB_G, w_gate_up[tile0, job], 2 * NT)
                if n == 0:
                    sp.wait_ge(res_ready, 16)
                    sp.dma_start(gain_row[:, :], gain_rows_in[2:3, :].to_broadcast((P, D))).then_inc(gain_landed, DMA)
                with sp.Fori(0, tiles - 1) as f:
                    for job in range(2):
                        for j in range(JOB_G):
                            load(g0 + (2 + job) * JOB_G + j, w_gate_up[f + (tile0 + 1), job, j], 2 * NT, f, 2 * JOB_G)
                g, k0, per_job = g0 + tiles * 2 * JOB_G, tile0 * F_CHUNKS // 2, tiles * F_CHUNKS // 2
                for job in range(4):
                    for j in range(per_job):
                        load(g + job * per_job + j, w_down[job, k0 + j], 2 * NT)
            for n in range(4):
                sp.wait_ge(out_ready, 2 * n + 2)
                sp.dma_start(out.rearrange("(t p) d -> p t d", p=P)[:, :, n * NT:(n + 1) * NT],
                             res[:, :, n * NT:(n + 1) * NT]).then_inc(out_stored, DMA)
            sp.wait_ge(out_stored, 4 * DMA)

        @block.tensor
        def _(pe):
            def use_granule(g, width, pair, hi, lo, chunk, first, last, it=0, per=0):
                slot = g % RING
                pe.wait_ge(lo_ready, it * per + (g + 1))
                for c in range(2):
                    cols = slice(c * width, (c + 1) * width)
                    for t in range(TT):
                        tile = acc[pair][t][:, 0:width]
                        x_hi = hi[:, chunk + c, t * P:(t + 1) * P]
                        x_lo = lo[:, chunk + c, t * P:(t + 1) * P]
                        nc.tensor.matmul(tile, x_hi, w_hi[:, slot, cols], start=first and c == 0, stop=False)
                        nc.tensor.matmul(tile, x_hi, w_lo[:, slot, cols], start=False, stop=False)
                        mm = nc.tensor.matmul(tile, x_lo, w_hi[:, slot, cols], start=False, stop=last and c == 1)
                mm.then_inc(granule_used, 1)

            def turn(bank, col, source):
                return nc.tensor.transpose(bank[:, col:col + P], source, ident[:, :])

            def level(bank, col, left, right):
                for t in range(TT):
                    ts = slice(t * P, (t + 1) * P)
                    mm = nc.tensor.matmul(bank[:, col + t * P:col + (t + 1) * P], left[:, ts], right[:, ts],
                                          start=True, stop=True)
                mm.then_inc(level_done, 1)

            def head_steps(pos, h):
                if pos == 0:
                    pe.wait_ge(acc_free[0], h * 4 + 2)
                    pe.wait_ge(acc_free[1], h * 2 + 2)
                    for i in range(2):
                        for t in range(TT):
                            mm = turn(s0, (2 * i + t) * P, proj_a[:, t, i * DH:(i + 1) * DH])
                    mm.then_inc(qk_turned, 1)
                    for t in range(TT):
                        turn(s1, t * P, proj_a[:, t, 3 * DH:4 * DH])
                    for t in range(TT):
                        mm = turn(s1, (2 + t) * P, proj_b[:, t, DH:2 * DH])
                    mm.then_inc(fz_turned, 1)
                if pos == 2:
                    pe.wait_ge(qk_copied, h + 1)
                    nc.tensor.matmul(s2[:, 0:SEQ], qk_t[:, P:2 * P], qk_t[:, 2 * P:4 * P], start=True, stop=True)
                    nc.tensor.matmul(s2[:, SEQ:SEQ + P], qk_t[:, 0:P], qk_t[:, 2 * P:3 * P],
                                     start=True, stop=True).then_inc(scores_done, 1)
                if pos == 5:
                    pe.wait_ge(prob_ready, h * 2 + 2)
                    pe.wait_ge(s3_copied, h + 1)
                    turn(s3, 0, prob[:, SEQ:SEQ + P])
                    turn(s3, P, prob[:, 0:P])
                    turn(s3, 2 * P, prob[:, P:2 * P]).then_inc(prob_turned, 1)
                if pos == 6:
                    pe.wait_ge(prob_t_ready, h + 1)
                    nc.tensor.matmul(s2[:, 0:SEQ], proj_a[:, 0, 2 * DH:3 * DH], prob_t[:, 0:SEQ],
                                     start=True, stop=False)
                    nc.tensor.matmul(s2[:, P:SEQ], proj_a[:, 1, 2 * DH:3 * DH], prob_t[:, SEQ:SEQ + P],
                                     start=False, stop=True).then_inc(pv_done, 1)
                if pos == 7:
                    pe.wait_ge(kk_ready, h + 1)
                    pe.wait_ge(qg_ready, h + 1)
                    level(s0, 0, kk, qg)
                    pe.wait_ge(factors_ready, h * 8 + 1)
                    level(s0, SEQ, decay[:, 0, :], decay[:, 0, :])
                if pos == 8:
                    for l, bank, col in ((1, s1, 0), (2, s1, SEQ), (3, s3, 0), (4, s3, SEQ)):
                        pe.wait_ge(factors_ready, h * 8 + (l + 1))
                        level(bank, col, decay[:, l, :], decay[:, l, :])
                if pos == 9:
                    pe.wait_ge(level_merged, h * 8 + 2)
                    for l, col in ((5, 0), (6, SEQ)):
                        pe.wait_ge(factors_ready, h * 8 + (l + 1))
                        level(s0, col, decay[:, l, :], decay[:, l, :])
                    pe.wait_ge(level_merged, h * 8 + 4)
                    pe.wait_ge(factors_ready, h * 8 + 8)
                    nc.tensor.matmul(s1[:, 0:P], decay[:, LEVELS, 0:P], decay[:, LEVELS, P:SEQ],
                                     start=True, stop=True).then_inc(cross_done, 1)
                if pos == 10:
                    pe.wait_ge(level_merged, h * 8 + 8)
                    pe.wait_ge(cross_copied, h + 1)
                    pe.wait_ge(attn_copied, h + 1)
                    nc.tensor.matmul(s2[:, 0:DH], att[:, 0:P], proj_b[:, 0, 0:DH], start=True, stop=True)
                    nc.tensor.matmul(s2[:, DH:2 * DH], att_x, proj_b[:, 0, 0:DH], start=True, stop=False)
                    nc.tensor.matmul(s2[:, DH:2 * DH], att[:, P:SEQ], proj_b[:, 1, 0:DH],
                                     start=False, stop=True).then_inc(o_done, 1)
                if pos == 12:
                    pe.wait_ge(y_ready, h + 1)
                    turn(s3, 0, y_hg[:, 0, :])
                    turn(s3, P, y_hg[:, 1, :]).then_inc(y_turned, 1)

            def turn_residual(k, n):
                if k == 0 and n == 0:
                    pe.wait_ge(s3_copied, HEADS + 1)
                pe.wait_ge(res_ready, 8 * k + 2 * n + 2)
                if n >= 2:
                    pe.wait_ge(a_lo_ready, 20 + 16 * k + 4 * (n - 1))
                for i in range(2):
                    for c in range(2):
                        for t in range(TT):
                            chunk = 4 * n + 2 * i + c
                            mm = turn(small[(2 * n + i) % 4], (2 * c + t) * P, res[:, t, chunk * P:(chunk + 1) * P])
                    mm.then_inc(res_turned, 1)

            def residual_operand(k, j):
                for n in {0: (0, 1), 2: (2,), 4: (3,)}.get(j, ()):
                    turn_residual(k, n)
                pe.wait_ge(a_lo_ready, 20 + 16 * k + 2 * j + 2)

            def cross_steps(pos, j):
                if pos == 0:
                    n = 4 + j
                    pe.wait_ge(acc_free[tail_pair(n)], 2 * tail_uses(n) + 2)
                    if j > 0:
                        pe.wait_ge(b_lo_ready, DC + 2 * j)
                    for i in range(2):
                        for c in range(2):
                            for t in range(TT):
                                chunk = 2 * i + c
                                mm = turn(small[i], (2 * c + t) * P, cq[:, t, chunk * P:(chunk + 1) * P])
                        mm.then_inc(cqk_turned, 1)
                    for i in range(2):
                        for c in range(2):
                            for m in range(TT):
                                col = j * CROSS_DH + (2 * i + c) * P
                                mm = turn(small[2 + i], (2 * c + m) * P, ckv[:, m, col:col + P])
                        mm.then_inc(cqk_turned, 1)
                if pos == 2:
                    pe.wait_ge(cqk_t_ready, 4 * j + 4)
                    for t in range(TT):
                        for c in range(CC):
                            mm = nc.tensor.matmul(s0[:, t * SEQ:(t + 1) * SEQ], cq_t[:, c, t * P:(t + 1) * P],
                                                  ck_t[:, c, :], start=c == 0, stop=c == CC - 1)
                    mm.then_inc(cscores_done, 1)
                if pos == 4:
                    pe.wait_ge(cprob_ready, j + 1)
                    for m in range(TT):
                        for t in range(TT):
                            mm = turn(s1, (2 * m + t) * P, cprob[:, t, m * P:(m + 1) * P])
                    mm.then_inc(cprob_turned, 1)
                if pos == 5:
                    pe.wait_ge(cprob_t_ready, j + 1)
                    for c in range(CC):
                        col = D + j * CROSS_DH + c * P
                        for m in range(TT):
                            mm = nc.tensor.matmul(small[2 + c // 2][:, (c % 2) * SEQ:(c % 2 + 1) * SEQ],
                                                  ckv[:, m, col:col + P], cprob_t[:, m, :], start=m == 0, stop=m == 1)
                        if c % 2:
                            mm.then_inc(cpv_done, 1)

            def turn_hidden(tile, uses):
                pe.wait_ge(acc_free[0], uses * 2 + 2)
                pe.wait_ge(b_lo_ready, tile * 2 + (DC + 8))
                for i in range(2):
                    for c in range(2):
                        for t in range(TT):
                            mm = turn(small[i], (2 * c + t) * P, hid[:, t, (2 * i + c) * P:(2 * i + c + 1) * P])
                    mm.then_inc(hid_turned, 1)

            pe.wait_ge(rel_landed, 2 * DMA)
            pe.wait_ge(rel_ones_set, 1)
            nc.tensor.matmul(s3[0:HEADS, 0:BETA], rel_sb, onehot, start=True, stop=True).then_inc(beta_done, 1)

            for j in range(JOB_G):
                pe.wait_ge(a_lo_ready, 2 * j + 2)
                use_granule(j, NT, 0, a_hi, a_lo, 2 * j, j == 0, j == JOB_G - 1)
            for j in range(JOB_G):
                use_granule(JOB_G + j, NB, 1, a_hi, a_lo, 2 * j, j == 0, j == JOB_G - 1)
                if j == 3:
                    pe.wait_ge(ident_landed, 2 * DMA)
                    pe.wait_ge(bias_landed, DMA)
                    pe.wait_ge(s3_copied, 1)
                    for i in range(4):
                        nc.tensor.matmul(small[i][:, :], flip, r1[:, i * 512:(i + 1) * 512],
                                         start=True, stop=True).then_inc(flip_done, 1)
            pe.wait_ge(bias_ready, 4)
            pe.wait_ge(b_lo_ready, DC)

            with pe.Fori(0, HEADS - 1) as h:
                pe.wait_ge(acc_free[0], h * 4 + 2)
                for j in range(JOB_G):
                    use_granule(G_BODY + j, NT, 0, b_hi, b_lo, 2 * j, j == 0, j == JOB_G - 1, h, BODY_G)
                    head_steps(j, h)
                pe.wait_ge(acc_free[0], h * 4 + 4)
                for j in range(JOB_G):
                    use_granule(G_BODY + JOB_G + j, NT, 0, a_hi, a_lo, 2 * j, j == 0, j == JOB_G - 1, h, BODY_G)
                    head_steps(JOB_G + j, h)
                pe.wait_ge(acc_free[1], h * 2 + 2)
                for j in range(JOB_G):
                    use_granule(G_BODY + 2 * JOB_G + j, NB, 1, a_hi, a_lo, 2 * j, j == 0, j == JOB_G - 1, h, BODY_G)

            last = HEADS - 1
            pe.wait_ge(acc_free[0], last * 4 + 2)
            for j in range(JOB_G):
                use_granule(G_LAST_HEAD + j, NT, 0, b_hi, b_lo, 2 * j, j == 0, j == JOB_G - 1)
                head_steps(j, last)

            def tail_job(n, g, granules, hi, lo, before=None, after=None):
                pe.wait_ge(acc_free[tail_pair(n)], 2 * tail_uses(n))
                for j in range(granules):
                    if before:
                        before(j)
                    use_granule(g + j, NT, tail_pair(n), hi, lo, 2 * j, j == 0, j == granules - 1)
                    if after:
                        after(j)

            def mix_split(j):
                pe.wait_ge(a_lo_ready, 17 if j < 3 else 18 if j < 7 else 20)

            tail_job(0, G_OUT, JOB_G, a_hi, a_lo, mix_split, lambda j: head_steps(JOB_G + j, last))
            for n in range(1, 4):
                tail_job(n, G_OUT + n * JOB_G, JOB_G, a_hi, a_lo)
            for j in range(CROSS_HEADS):
                tail_job(4 + j, G_CQ + j * JOB_G, JOB_G, a_hi, a_lo,
                         None if j else (lambda k: residual_operand(0, k)),
                         (lambda k: cross_steps(k, j - 1)) if j else None)
            tail_job(8, G_CO, JOB_G, b_hi, b_lo, lambda k: pe.wait_ge(b_lo_ready, DC + k + 1),
                     lambda k: cross_steps(k, CROSS_HEADS - 1))
            for n in range(1, 4):
                tail_job(8 + n, G_CO + n * JOB_G, JOB_G, b_hi, b_lo)
            for tile0, tiles, g0, n0 in groups:
                tail_job(n0, g0, JOB_G, a_hi, a_lo, None if tile0 else (lambda k: residual_operand(1, k)))
                tail_job(n0 + 1, g0 + JOB_G, JOB_G, a_hi, a_lo)
                with pe.Fori(0, tiles - 1) as f:
                    pe.wait_ge(acc_free[1], f * 2 + (2 * tail_uses(n0) + 2))
                    for j in range(JOB_G):
                        use_granule(g0 + 2 * JOB_G + j, NT, 1, a_hi, a_lo, 2 * j, j == 0, j == JOB_G - 1, f, 2 * JOB_G)
                        if j == 1:
                            turn_hidden(f + tile0, f + tail_uses(n0 + 1))
                    pe.wait_ge(acc_free[0], f * 2 + (2 * tail_uses(n0 + 1) + 2))
                    for j in range(JOB_G):
                        use_granule(g0 + 3 * JOB_G + j, NT, 0, a_hi, a_lo, 2 * j, j == 0, j == JOB_G - 1, f, 2 * JOB_G)
                per_job = tiles * F_CHUNKS // 2
                g1, n1 = g0 + tiles * 2 * JOB_G, n0 + 2 * tiles
                for m in range(4):
                    tail_job(n1 + m, g1 + m * per_job, per_job, b_hi, b_lo,
                             (lambda k: pe.wait_ge(b_lo_ready, DC + 8 + 2 * tile0 + k + 1)) if m == 0 else None,
                             (lambda k: turn_hidden(tile0 + tiles - 1, tail_uses(n1 - 1)) if k == 1 else None)
                             if m == 0 else None)

        @block.scalar
        def _(act):
            def split_hi(g, width=2 * NT, it=0, per=0):
                slot = g % RING
                act.wait_ge(raw_landed[slot], it * (per // RING * DMA) + (g // RING + 1) * DMA)
                if g >= RING:
                    act.wait_ge(granule_used, it * per + (g - RING + 1))
                nc.scalar.activation(w_hi[:, slot, 0:width], raw[:, slot, 0:width], ACT.Copy).then_inc(hi_ready, 1)

            def rstd(squares, to, count):
                act.wait_ge(squares_ready, count)
                nc.scalar.activation(to, squares, ACT.Ln, scale=1.0 / D, bias=eps_col).then_inc(log_ready, 1)
                act.wait_ge(log_ready, count)
                nc.scalar.activation(to, to, ACT.Exp, scale=-0.5).then_inc(rstd_ready, 1)

            def copy_out(used, bank, to, scale, pair):
                act.wait_ge(granule_used, used)
                nc.scalar.activation(to, bank, ACT.Copy, scale=scale).then_inc(acc_free[pair], 1)

            def head_steps(pos, h, used):
                if pos == 2:
                    copy_out(used, acc[1][0][:, 0:NB], proj_b[:, 0, :], rstd_x[:, 0:1], 1)
                if pos == 4:
                    act.wait_ge(qk_turned, h + 1)
                    nc.scalar.activation(qk_t, s0[:, :], ACT.Copy).then_inc(qk_copied, 1)
                    act.wait_ge(fz_turned, h + 1)
                    nc.scalar.activation(sig, s1[:, :], ACT.Sigmoid).then_inc(sig_ready, 1)
                    act.wait_ge(acc_free[1], h * 2 + 2)
                    nc.scalar.activation(gsil, proj_b[:, :, 2 * DH:3 * DH], ACT.Sigmoid).then_inc(gz_sig, 1)
                    nc.scalar.preload_act_table_set("natural_log_exp_and_others")
                    act.wait_ge(sig_ready, h + 1)
                    nc.scalar.activation(logf, sig[:, 0:SEQ], ACT.Ln).then_inc(logf_ready, 1)
                if pos == 6:
                    act.wait_ge(max_ready, h * 2 + 2)
                    nc.scalar.activation(prob[:, 0:SEQ], prob[:, 0:SEQ], ACT.Exp, bias=neg_max[:, 1:2],
                                         accum_out=row_sum[:, 1:2])
                    nc.scalar.activation(prob[:, SEQ:SEQ + P], prob[:, SEQ:SEQ + P], ACT.Exp, bias=neg_max[:, 0:1],
                                         accum_out=row_sum[:, 0:1]).then_inc(prob_exp, 1)
                if pos == 8:
                    act.wait_ge(prob_turned, h + 1)
                    nc.scalar.activation(prob_t, s3[:, 0:BETA], ACT.Copy).then_inc(prob_t_ready, 1)
                    act.wait_ge(decay_log, h * 8 + 4)
                    nc.scalar.activation(decay[:, 0:4, :], decay[:, 0:4, :], ACT.Exp).then_inc(decay_ready, 1)
                if pos == 9:
                    act.wait_ge(decay_log, h * 8 + 8)
                    nc.scalar.activation(decay[:, 4:8, :], decay[:, 4:8, :], ACT.Exp).then_inc(decay_ready, 1)
                if pos == 10:
                    act.wait_ge(pv_done, h + 1)
                    nc.scalar.activation(mix_t[:, attn_chunk(h), :], s2[:, 0:SEQ], ACT.Copy).then_inc(attn_copied, 1)
                    copy_out(used + JOB_G, acc[0][0][:, :], ckv[:, 0, bass.ds(h * NT, NT)], rstd_m[:, 0:1], 0)
                if pos == 12:
                    act.wait_ge(cross_done, h + 1)
                    nc.scalar.activation(att_x, s1[:, 0:P], ACT.Copy).then_inc(cross_copied, 1)
                if pos == 13:
                    act.wait_ge(o_done, h + 1)
                    nc.scalar.activation(junk[:, 0, 0:DH], s2[:, 0:DH], ACT.Square, accum_out=ssq_o[:, 0:1])
                    nc.scalar.activation(junk[:, 1, 0:DH], s2[:, DH:2 * DH], ACT.Square,
                                         accum_out=ssq_o[:, 1:2]).then_inc(o_squared, 1)
                    act.wait_ge(o_squared, h + 1)
                    nc.scalar.activation(rstd_o, ssq_o, ACT.Ln, scale=1.0 / DH, bias=eps_col).then_inc(o_log, 1)
                    act.wait_ge(o_log, h + 1)
                    nc.scalar.activation(rstd_o, rstd_o, ACT.Exp, scale=-0.5).then_inc(o_rstd, 1)
                if pos == 16:
                    act.wait_ge(y_turned, h + 1)
                    gain = hg_gain[:, h:h + 1] if isinstance(h, int) else hg_gain[:, bass.ds(h, 1)]
                    nc.scalar.activation(mix_t[:, hg_chunk(h), :], s3[:, 0:SEQ], ACT.Copy,
                                         scale=gain).then_inc(s3_copied, 1)

            def square_sub(n, m, used, k):
                pair = tail_pair(n)
                act.wait_ge(granule_used, used)
                nc.scalar.activation(junk[:, 2 * pair + 1, :], acc[pair][1][:, :], ACT.Square,
                                     accum_out=ssq_n[:, 1, m:m + 1]).then_inc(sub1_squared, 1)
                act.wait_ge(sub0_scaled, 4 * k + m + 1)
                nc.scalar.activation(junk[:, 2 * pair, :], acc[pair][0][:, :], ACT.Square,
                                     accum_out=ssq_n[:, 0, m:m + 1]).then_inc(acc_free[pair], 1)

            def next_operand(k):
                rstd(ssq, rstd_n, NORM_OUT + 2 * k)
                for n in range(4):
                    for i in range(2):
                        act.wait_ge(res_turned, 8 * k + 2 * n + i + 1)
                        for c in range(2):
                            chunk = 4 * n + 2 * i + c
                            nc.scalar.activation(a_hi[:, chunk, :], small[(2 * n + i) % 4][:, c * SEQ:(c + 1) * SEQ],
                                                 ACT.Copy, scale=gcol[:, 2 + k, chunk:chunk + 1]).then_inc(a_hi_ready, 1)
                for n in range(4):
                    for t in range(TT):
                        done = 8 * k + 2 * n + t
                        if done >= 4:
                            act.wait_ge(res_squared, done - 3)
                        nc.scalar.activation(junk[:, done % 4, :], res[:, t, n * NT:(n + 1) * NT], ACT.Square,
                                             accum_out=ssq_r[:, t, n:n + 1]).then_inc(res_squared, 1)
                rstd(ssq, rstd_r, NORM_CQ + 2 * k)

            def cross_steps(pos, j, used):
                if pos == 2:
                    n = 4 + j
                    copy_out(used, acc[tail_pair(n)][0][:, :], cq[:, 0, :], rstd_r[:, 0:1], tail_pair(n))
                if pos == 3:
                    act.wait_ge(cqk_turned, 4 * j + 1)
                    nc.scalar.activation(cq_t[:, 0:2, :], s0[:, :], ACT.Copy).then_inc(cqk_t_ready, 1)
                    act.wait_ge(cqk_turned, 4 * j + 3)
                    nc.scalar.activation(ck_t[:, 0:2, :], s2[:, :], ACT.Copy).then_inc(cqk_t_ready, 1)
                if pos == 5:
                    act.wait_ge(cbias_ready, j + 1)
                    for t in range(TT):
                        e = nc.scalar.activation(cprob[:, t, :], s0[:, t * SEQ:(t + 1) * SEQ], ACT.Exp,
                                                 scale=CROSS_DH ** -0.5, bias=neg_max[:, t:t + 1],
                                                 accum_out=row_sum[:, t:t + 1])
                    e.then_inc(cprob_exp, 1)
                if pos == 7:
                    act.wait_ge(cprob_turned, j + 1)
                    nc.scalar.activation(cprob_t, s1[:, :], ACT.Copy).then_inc(cprob_t_ready, 1)
                if pos == 8:
                    for i in range(2):
                        act.wait_ge(cpv_done, 2 * j + i + 1)
                        nc.scalar.activation(b_hi[:, 4 * j + 2 * i:4 * j + 2 * i + 2, :], small[2 + i][:, :],
                                             ACT.Copy).then_inc(b_hi_ready, 1)

            def silu_gate(used):
                act.wait_ge(granule_used, used)
                for t in range(TT):
                    nc.scalar.activation(gs[:, t, :], acc[1][t][:, :], ACT.Silu,
                                         scale=rstd_r[:, t:t + 1]).then_inc(acc_free[1], 1)

            def hidden_hi(tile, ft):
                for i in range(2):
                    act.wait_ge(hid_turned, tile * 2 + (i + 1))
                    nc.scalar.activation(b_hi[:, bass.ds(ft * F_CHUNKS + 2 * i, 2), :], small[i][:, :],
                                         ACT.Copy).then_inc(b_hi_ready, 1)

            def act_down(i, m, used):
                n = groups[i][3] + 2 * groups[i][1] + m
                pair, cols = tail_pair(n), slice(m * NT, (m + 1) * NT)
                if i == 0:
                    copy_out(used, acc[pair][0][:, :], sub[:, 0, cols], 1.0, pair)
                if i == 2:
                    act.wait_ge(acc_free[pair], 2 * tail_uses(n) + 2)
                    if m:
                        act.wait_ge(y_squared, m)
                    for t in range(TT):
                        sq = nc.scalar.activation(junk[:, 2 * pair + t, :], sub[:, t, cols], ACT.Square,
                                                  accum_out=ssq_n[:, t, m:m + 1])
                    sq.then_inc(y_squared, 1)

            act.dma_start(rel_sb[0:REL_BUCKETS, :], rel_bias).then_inc(rel_landed, DMA)
            act.dma_start(onehot, onehot_in).then_inc(rel_landed, DMA)
            nc.scalar.preload_act_table_set("natural_log_exp_and_others")
            act.wait_ge(gcol_landed, DMA)
            act.wait_ge(consts_set, 1)
            for pos in range(G_BODY):
                split_hi(pos, 2 * (NT if pos < JOB_G else NB))
                if pos < JOB_G:
                    act.wait_ge(xt_landed[pos], DMA)
                    for c in (2 * pos, 2 * pos + 1):
                        nc.scalar.activation(a_hi[:, c, :], x_t[:, c, :], ACT.Copy,
                                             scale=gcol[:, 0, c:c + 1]).then_inc(a_hi_ready, 1)
                else:
                    if pos == JOB_G:
                        act.wait_ge(memt_landed, DMA)
                    for c in (2 * (pos - JOB_G), 2 * (pos - JOB_G) + 1):
                        nc.scalar.activation(b_hi[:, c, :], mem_t[:, c, :], ACT.Copy,
                                             scale=gcol[:, 1, c:c + 1]).then_inc(b_hi_ready, 1)
                if pos == 0:
                    act.dma_start(mem_nat, mem.rearrange("(t p) d -> p t d", p=P)).then_inc(mem_landed, DMA)
                    act.dma_start(x_nat, x.rearrange("(t p) d -> p t d", p=P)).then_inc(x_landed, DMA)
                if pos == 1:
                    act.wait_ge(beta_done, 1)
                    nc.scalar.activation(beta_sb, s3[0:HEADS, 0:BETA], ACT.Copy).then_inc(s3_copied, 1)
                    act.dma_start(mem_t, memt.rearrange("(c p) s -> p c s", p=P)).then_inc(memt_landed, DMA)
                if pos == 2:
                    act.wait_ge(s3_copied, 1)
                    act.dma_start(beta_dram, beta_sb).then_inc(beta_stored, DMA)
                    act.dma_start(ident[:, :], ident_in).then_inc(ident_landed, DMA)
                    act.dma_start(flip, flip_in).then_inc(ident_landed, DMA)
                    act.dma_start(masks_wide, masks_in).then_inc(const_landed, DMA)
                    act.dma_start(hg_gain[:, :], hg_gain_in).then_inc(const_landed, DMA)
                if pos == 7:
                    for nat, landed, squares, to, count in ((mem_nat, mem_landed, ssq_m, rstd_m, NORM_MEM),
                                                            (x_nat, x_landed, ssq, rstd_x, NORM_X)):
                        act.wait_ge(landed, DMA)
                        for t in range(TT):
                            sq = nc.scalar.activation(nat[:, t, :], nat[:, t, :], ACT.Square,
                                                      accum_out=squares[:, t:t + 1])
                        sq.then_inc(squares_ready, 1)
                        rstd(squares, to, count)
                if pos == 9:
                    act.wait_ge(beta_stored, DMA)
                    act.dma_start(bias_rev, bass.AP(tensor=beta_dram.tensor, offset=beta_dram.offset,
                                                    ap=[[1, P], [BETA, HEADS], [1, SEQ]])).then_inc(bias_landed, DMA)
                if pos == 14:
                    for i in range(2):
                        act.wait_ge(flip_done, i + 1)
                        nc.scalar.activation(r4[:, i * 512:(i + 1) * 512], small[i][:, :], ACT.Copy).then_inc(bias_ready, 1)
                if pos == 10:
                    act.wait_ge(rstd_ready, NORM_X)
                    copy_out(JOB_G, acc[0][0][:, :], proj_a[:, 0, :], rstd_x[:, 0:1], 0)
            act.wait_ge(const_landed, 2 * DMA)

            with act.Fori(0, HEADS - 1) as h:
                for pos in range(BODY_G):
                    split_hi(G_BODY + pos, 2 * (NT if pos < 2 * JOB_G else NB), h, BODY_G)
                    head_steps(pos, h, h * BODY_G + G_BODY)
                    if pos == 2 * JOB_G + 2:
                        copy_out(h * BODY_G + (G_BODY + 2 * JOB_G), acc[0][0][:, :], proj_a[:, 0, :], rstd_x[:, 0:1], 0)

            q_cq, q_ffn = G_CQ - G_LAST_HEAD, G_FFN - G_LAST_HEAD
            for q in range(q_ffn + 4):
                split_hi(G_LAST_HEAD + q)
                head_steps(q, HEADS - 1, G_LAST_HEAD)
                if q in (5, 6):
                    c0 = 7 * (q - 5)
                    act.wait_ge(s3_copied, HEADS)
                    nc.scalar.activation(a_hi[:, c0:c0 + 7, :], mix_t[:, c0:c0 + 7, :], ACT.Copy).then_inc(a_hi_ready, 1)
                if q == 11:
                    act.wait_ge(attn_copied, HEADS)
                    nc.scalar.activation(a_hi[:, 14, :], mix_t[:, 14, :], ACT.Copy).then_inc(a_hi_ready, 1)
                if q == 16:
                    act.wait_ge(s3_copied, HEADS + 1)
                    nc.scalar.activation(a_hi[:, 15, :], mix_t[:, 15, :], ACT.Copy).then_inc(a_hi_ready, 1)
                for k, start, n0 in ((0, q_cq, 0), (1, q_ffn, 8)):
                    for m in range(4):
                        if q == start - (3 - m) * JOB_G + (2 if m < 3 else 3):
                            square_sub(n0 + m, m, G_LAST_HEAD + start - (3 - m) * JOB_G, k)
                            if m == 3:
                                next_operand(k)
                for j in range(CROSS_HEADS):
                    cross_steps(q - q_cq - (j + 1) * JOB_G, j, G_CQ + (j + 1) * JOB_G)
            act.wait_ge(rstd_ready, NORM_FFN)
            nc.scalar.preload_act_table(ACT.Silu)

            for i, (tile0, tiles, g0, n0) in enumerate(groups):
                for pos in range(4 if i == 0 else 0, 2 * JOB_G):
                    split_hi(g0 + pos)
                    if i and pos == 2:
                        act_down(i - 1, 3, g0)
                    if pos == 10:
                        silu_gate(g0 + JOB_G)
                with act.Fori(0, tiles - 1) as f:
                    for pos in range(2 * JOB_G):
                        split_hi(g0 + 2 * JOB_G + pos, 2 * NT, f, 2 * JOB_G)
                        if pos == 4:
                            hidden_hi(f + tile0, f)
                        if pos == 10:
                            silu_gate(f * (2 * JOB_G) + (g0 + 3 * JOB_G))
                per_job = tiles * F_CHUNKS // 2
                g1, n1 = g0 + tiles * 2 * JOB_G, n0 + 2 * tiles
                for pos in range(4 * per_job):
                    split_hi(g1 + pos)
                    if pos == 4:
                        hidden_hi(tile0 + tiles - 1, tiles - 1)
                    for m in range(3):
                        if pos == (m + 1) * per_job + 2:
                            act_down(i, m, g1 + (m + 1) * per_job)
            act_down(2, 3, 0)
            nc.scalar.preload_act_table_set("natural_log_exp_and_others")
            rstd(ssq, rstd_n, NORM_Y)

        @block.vector
        def _(dve):
            def split_lo(g, width=2 * NT, it=0, per=0):
                slot = g % RING
                dve.wait_ge(hi_ready, it * per + (g + 1))
                nc.vector.tensor_tensor(w_lo[:, slot, 0:width], raw[:, slot, 0:width],
                                        w_hi[:, slot, 0:width].bitcast(F32), ALU.subtract).then_inc(lo_ready, 1)

            def copy_out(used, bank, to, scale, pair):
                dve.wait_ge(granule_used, used)
                nc.vector.tensor_scalar(to, bank, scale, None, ALU.mult).then_inc(acc_free[pair], 1)

            def masked_pairs(l, bank, col):
                return (att.rearrange("p (t n) -> p t n", t=TT), masks[:, l, :].unsqueeze(1).to_broadcast((P, TT, P)),
                        bank[:, col:col + SEQ].rearrange("p (t n) -> p t n", t=TT))

            def merge(h, k, l, bank, col):
                dve.wait_ge(level_done, h * 8 + (k // 2 * 2 + 2))
                dve.wait_ge(level_merged, h * 8 + k)
                dve.nop(nofuse=True)
                nc.vector.copy_predicated(*masked_pairs(l, bank, col)).then_inc(level_merged, 1)

            def factors(h, l):
                m = 1 << l
                halves = decay[:, l, :].rearrange("p (n x m) -> p n x m", x=2, m=m)
                k_halves = kk.rearrange("p (n x m) -> p n x m", x=2, m=m)
                q_halves = qg.rearrange("p (n x m) -> p n x m", x=2, m=m)
                nc.vector.tensor_tensor(halves[:, :, 0, :], halves[:, :, 0, :], k_halves[:, :, 0, :], ALU.mult)
                nc.vector.tensor_tensor(halves[:, :, 1, :], halves[:, :, 1, :], q_halves[:, :, 1, :],
                                        ALU.mult).then_inc(factors_ready, 1)

            def head_steps(pos, h, used):
                if pos == 2:
                    copy_out(used, acc[1][1][:, 0:NB], proj_b[:, 1, :], rstd_x[:, 1:2], 1)
                if pos == 4:
                    dve.wait_ge(sig_ready, h + 1)
                    nc.vector.tensor_scalar(kk, sig[:, 0:SEQ], -1.0, 1.0, ALU.mult, ALU.add).then_inc(kk_ready, 1)
                    nc.vector.tensor_tensor(qg, s1[:, SEQ:2 * SEQ], sig[:, SEQ:2 * SEQ], ALU.mult).then_inc(qg_ready, 1)
                if pos == 5:
                    dve.wait_ge(logf_ready, h + 1)
                    for t in range(TT):
                        ts = slice(t * P, (t + 1) * P)
                        scan = nc.vector.tensor_tensor_scan(b[:, ts], ones[:, :], logf[:, ts], 0.0, ALU.mult, ALU.add)
                    scan.then_inc(b_ready, 1)
                    dve.wait_ge(scores_done, h + 1)
                    bias_h = bias[:, h, :]
                    nc.vector.scalar_tensor_tensor(prob[:, 0:SEQ], s2[:, 0:SEQ], DH ** -0.5, bias_h,
                                                   ALU.mult, ALU.add)
                    nc.vector.scalar_tensor_tensor(prob[:, SEQ:SEQ + P], s2[:, SEQ:SEQ + P], DH ** -0.5,
                                                   bias[:, h, P:SEQ], ALU.mult, ALU.add).then_inc(logits_ready, 1)
                    dve.wait_ge(logits_ready, h + 1)
                    nc.vector.tensor_reduce(neg_max[:, 1:2], prob[:, 0:SEQ], AX.X, ALU.max,
                                            negate=True).then_inc(max_ready, 1)
                    nc.vector.tensor_reduce(neg_max[:, 0:1], prob[:, SEQ:SEQ + P], AX.X, ALU.max,
                                            negate=True).then_inc(max_ready, 1)
                if pos == 7:
                    dve.wait_ge(prob_exp, h + 1)
                    nc.vector.reciprocal(row_sum, row_sum).then_inc(sum_inv, 1)
                    dve.wait_ge(sum_inv, h + 1)
                    nc.vector.tensor_scalar(prob[:, 0:SEQ], prob[:, 0:SEQ], row_sum[:, 1:2], None,
                                            ALU.mult).then_inc(prob_ready, 1)
                    nc.vector.tensor_scalar(prob[:, SEQ:SEQ + P], prob[:, SEQ:SEQ + P], row_sum[:, 0:1], None,
                                            ALU.mult).then_inc(prob_ready, 1)
                if pos == 8:
                    dve.wait_ge(gz_sig, h + 1)
                    nc.vector.tensor_tensor(gsil, gsil, proj_b[:, :, 2 * DH:3 * DH], ALU.mult).then_inc(gz_silu, 1)
                if pos == 9:
                    dve.wait_ge(decay_ready, h * 2 + 1)
                    for l in range(4):
                        factors(h, l)
                if pos == 10:
                    copy_out(used + JOB_G, acc[0][1][:, :], ckv[:, 1, bass.ds(h * NT, NT)], rstd_m[:, 1:2], 0)
                    dve.wait_ge(decay_ready, h * 2 + 2)
                    for l in range(4, 7):
                        factors(h, l)
                    nc.vector.tensor_tensor(decay[:, LEVELS, 0:P], decay[:, LEVELS, 0:P], kk[:, 0:P], ALU.mult)
                    nc.vector.tensor_tensor(decay[:, LEVELS, P:SEQ], decay[:, LEVELS, P:SEQ], qg[:, P:SEQ],
                                            ALU.mult).then_inc(factors_ready, 1)
                if pos == 11:
                    dve.wait_ge(level_done, h * 8 + 2)
                    nc.vector.tensor_tensor(att.rearrange("p (t n) -> p t n", t=TT),
                                            s0[:, 0:SEQ].rearrange("p (t n) -> p t n", t=TT),
                                            ident[:, :].unsqueeze(1).to_broadcast((P, TT, P)),
                                            ALU.mult).then_inc(level_merged, 1)
                    merge(h, 1, 0, s0, SEQ)
                if pos == 12:
                    merge(h, 2, 1, s1, 0)
                    merge(h, 3, 2, s1, SEQ)
                    merge(h, 4, 3, s3, 0)
                if pos == 13:
                    merge(h, 5, 4, s3, SEQ)
                    merge(h, 6, 5, s0, 0)
                    merge(h, 7, 6, s0, SEQ)
                if pos == 15:
                    dve.wait_ge(o_rstd, h + 1)
                    for t in range(TT):
                        y = nc.vector.scalar_tensor_tensor(y_hg[:, t, :], s2[:, t * DH:(t + 1) * DH],
                                                           rstd_o[:, t:t + 1], gsil[:, t, :], ALU.mult, ALU.mult)
                    y.then_inc(y_ready, 1)

            def gain_sub(n, m, used, k):
                pair = tail_pair(n)
                dve.wait_ge(gain_landed, (k + 1) * DMA)
                dve.wait_ge(granule_used, used)
                cols = slice(m * NT, (m + 1) * NT)
                nc.vector.tensor_tensor(sub[:, 0, cols], acc[pair][0][:, :], gain_row[:, cols],
                                        ALU.mult).then_inc(sub0_scaled, 1)
                dve.wait_ge(sub1_squared, 4 * k + m + 1)
                nc.vector.tensor_tensor(sub[:, 1, cols], acc[pair][1][:, :], gain_row[:, cols],
                                        ALU.mult).then_inc(acc_free[pair], 1)

            def next_operand(k, n3):
                for n in (n3 - 1, n3):
                    dve.wait_ge(acc_free[tail_pair(n)], 2 * tail_uses(n) + 2)
                nc.vector.tensor_reduce(ssq, ssq_n, AX.X, ALU.add).then_inc(squares_ready, 1)
                if k == 0:
                    dve.wait_ge(res_landed, DMA)
                dve.wait_ge(rstd_ready, NORM_OUT + 2 * k)

                def residual(n):
                    for t in range(TT):
                        cols = slice(n * NT, (n + 1) * NT)
                        nc.vector.scalar_tensor_tensor(res[:, t, cols], sub[:, t, cols], rstd_n[:, t:t + 1],
                                                       res[:, t, cols], ALU.mult, ALU.add).then_inc(res_ready, 1)

                def operand_lo(n):
                    for chunk in range(4 * n, 4 * n + 4):
                        i, c = (chunk - 4 * n) // 2, chunk % 2
                        dve.wait_ge(a_hi_ready, 20 + 16 * k + (chunk | 1) + 1)
                        nc.vector.scalar_tensor_tensor(a_lo[:, chunk, :],
                                                       small[(2 * n + i) % 4][:, c * SEQ:(c + 1) * SEQ],
                                                       gcol[:, 2 + k, chunk:chunk + 1],
                                                       a_hi[:, chunk, :].bitcast(F32),
                                                       ALU.mult, ALU.subtract).then_inc(a_lo_ready, 1)

                residual(0)
                for n in range(1, 4):
                    residual(n)
                    operand_lo(n - 1)
                operand_lo(3)
                dve.wait_ge(res_squared, 8 * k + 8)
                nc.vector.tensor_reduce(ssq, ssq_r, AX.X, ALU.add).then_inc(squares_ready, 1)
                dve.wait_ge(rstd_ready, NORM_CQ + 2 * k)

            def cross_steps(pos, j, used):
                if pos == 2:
                    n = 4 + j
                    copy_out(used, acc[tail_pair(n)][1][:, :], cq[:, 1, :], rstd_r[:, 1:2], tail_pair(n))
                if pos == 3:
                    dve.wait_ge(cqk_turned, 4 * j + 2)
                    nc.vector.tensor_copy(cq_t[:, 2:4, :], s1[:, :].rearrange("p (c s) -> p c s", c=2)).then_inc(cqk_t_ready, 1)
                    dve.wait_ge(cqk_turned, 4 * j + 4)
                    nc.vector.tensor_copy(ck_t[:, 2:4, :], s3[:, :].rearrange("p (c s) -> p c s", c=2)).then_inc(cqk_t_ready, 1)
                if pos == 5:
                    dve.wait_ge(cscores_done, j + 1)
                    nc.vector.tensor_reduce(neg_max, s0[:, :].rearrange("p (t m) -> p t m", t=TT), AX.X, ALU.max,
                                            negate=True).then_inc(cmax_ready, 1)
                    dve.wait_ge(cmax_ready, j + 1)
                    nc.vector.tensor_scalar(neg_max, neg_max, CROSS_DH ** -0.5, None, ALU.mult).then_inc(cbias_ready, 1)
                if pos == 6:
                    dve.wait_ge(cprob_exp, j + 1)
                    nc.vector.reciprocal(row_sum, row_sum).then_inc(csum_inv, 1)
                    dve.wait_ge(csum_inv, j + 1)
                    for t in range(TT):
                        p = nc.vector.tensor_scalar(cprob[:, t, :], cprob[:, t, :], row_sum[:, t:t + 1], None, ALU.mult)
                    p.then_inc(cprob_ready, 1)
                if pos == 9:
                    for i in range(2):
                        dve.wait_ge(b_hi_ready, DC + 2 * j + i + 1)
                        pair = slice(4 * j + 2 * i, 4 * j + 2 * i + 2)
                        nc.vector.tensor_tensor(b_lo[:, pair, :], small[2 + i][:, :].rearrange("p (c s) -> p c s", c=2),
                                                b_hi[:, pair, :].bitcast(F32), ALU.subtract).then_inc(b_lo_ready, 1)

            def hidden(used, gate_uses):
                dve.wait_ge(granule_used, used)
                dve.wait_ge(acc_free[1], gate_uses * 2 + 2)
                for t in range(TT):
                    nc.vector.scalar_tensor_tensor(hid[:, t, :], acc[0][t][:, :], rstd_r[:, t:t + 1], gs[:, t, :],
                                                   ALU.mult, ALU.mult).then_inc(acc_free[0], 1)

            def hidden_lo(tile, ft):
                for i in range(2):
                    dve.wait_ge(b_hi_ready, tile * 2 + (DC + 8 + i + 1))
                    pair = bass.ds(ft * F_CHUNKS + 2 * i, 2)
                    nc.vector.tensor_tensor(b_lo[:, pair, :], small[i][:, :].rearrange("p (c s) -> p c s", c=2),
                                            b_hi[:, pair, :].bitcast(F32), ALU.subtract).then_inc(b_lo_ready, 1)

            def down(i, m, used):
                n = groups[i][3] + 2 * groups[i][1] + m
                pair, cols = tail_pair(n), slice(m * NT, (m + 1) * NT)
                dve.wait_ge(granule_used, used)
                if i == 0:
                    nc.vector.tensor_copy(sub[:, 1, cols], acc[pair][1][:, :]).then_inc(acc_free[pair], 1)
                    return
                before = groups[i - 1][3] + 2 * groups[i - 1][1] + m
                dve.wait_ge(acc_free[tail_pair(before)], 2 * tail_uses(before) + 2)
                for t in range(TT):
                    nc.vector.tensor_tensor(sub[:, t, cols], acc[pair][t][:, :], sub[:, t, cols],
                                            ALU.add).then_inc(acc_free[pair], 1)
                if i == 2:
                    dve.wait_ge(gain_landed, 3 * DMA)
                    dve.wait_ge(acc_free[pair], 2 * tail_uses(n) + 2)
                    for t in range(TT):
                        nc.vector.tensor_tensor(yg[:, t, cols], sub[:, t, cols], gain_row[:, cols],
                                                ALU.mult).then_inc(yg_ready, 1)

            dve.wait_ge(gcol_landed, DMA)
            for pos in range(G_BODY):
                split_lo(pos, 2 * (NT if pos < JOB_G else NB))
                source, hi, lo, hi_count, lo_count, norm, c0 = (
                    (x_t, a_hi, a_lo, a_hi_ready, a_lo_ready, 0, 2 * pos) if pos < JOB_G else
                    (mem_t, b_hi, b_lo, b_hi_ready, b_lo_ready, 1, 2 * (pos - JOB_G)))
                for c in (c0, c0 + 1):
                    dve.wait_ge(hi_count, c + 1)
                    nc.vector.scalar_tensor_tensor(lo[:, c, :], source[:, c, :], gcol[:, norm, c:c + 1],
                                                   hi[:, c, :].bitcast(F32), ALU.mult, ALU.subtract).then_inc(lo_count, 1)
                if pos == 14:
                    for i in range(2, 4):
                        dve.wait_ge(flip_done, i + 1)
                        nc.vector.tensor_copy(r4[:, i * 512:(i + 1) * 512], small[i][:, :]).then_inc(bias_ready, 1)
                if pos == 10:
                    dve.wait_ge(rstd_ready, NORM_X)
                    copy_out(JOB_G, acc[0][1][:, :], proj_a[:, 1, :], rstd_x[:, 1:2], 0)
            dve.wait_ge(const_landed, 2 * DMA)
            nc.vector.tensor_copy(masks[:, :, :], masks_wide).then_inc(masks_ready, 1)
            dve.wait_ge(masks_ready, 1)
            dve.wait_ge(ident_landed, 2 * DMA)
            dve.wait_ge(bias_ready, 4)
            dve.wait_ge(consts_set, 1)

            with dve.Fori(0, HEADS - 1) as h:
                for pos in range(BODY_G):
                    split_lo(G_BODY + pos, 2 * (NT if pos < 2 * JOB_G else NB), h, BODY_G)
                    head_steps(pos, h, h * BODY_G + G_BODY)
                    if pos == 2 * JOB_G + 2:
                        copy_out(h * BODY_G + (G_BODY + 2 * JOB_G), acc[0][1][:, :], proj_a[:, 1, :], rstd_x[:, 1:2], 0)

            q_cq, q_ffn = G_CQ - G_LAST_HEAD, G_FFN - G_LAST_HEAD
            for q in range(q_ffn + 4):
                split_lo(G_LAST_HEAD + q)
                head_steps(q, HEADS - 1, G_LAST_HEAD)
                for at, chunks in ((6, slice(0, 7)), (7, slice(7, 14)), (12, slice(14, 15)), (16, slice(15, 16))):
                    if q == at:
                        dve.wait_ge(a_hi_ready, DC + 1 + (6, 7, 12, 16).index(at))
                        nc.vector.tensor_tensor(a_lo[:, chunks, :], mix_t[:, chunks, :], a_hi[:, chunks, :].bitcast(F32),
                                                ALU.subtract).then_inc(a_lo_ready, 1)
                for k, start, n0 in ((0, q_cq, 0), (1, q_ffn, 8)):
                    for m in range(4):
                        if q == start - (3 - m) * JOB_G + (2 if m < 3 else 3):
                            gain_sub(n0 + m, m, G_LAST_HEAD + start - (3 - m) * JOB_G, k)
                            if m == 3:
                                next_operand(k, n0 + 3)
                for j in range(CROSS_HEADS):
                    cross_steps(q - q_cq - (j + 1) * JOB_G, j, G_CQ + (j + 1) * JOB_G)

            for i, (tile0, tiles, g0, n0) in enumerate(groups):
                for pos in range(4 if i == 0 else 0, 2 * JOB_G):
                    split_lo(g0 + pos)
                    if i and pos == 2:
                        down(i - 1, 3, g0)
                with dve.Fori(0, tiles - 1) as f:
                    for pos in range(2 * JOB_G):
                        split_lo(g0 + 2 * JOB_G + pos, 2 * NT, f, 2 * JOB_G)
                        if pos == 2:
                            hidden(f * (2 * JOB_G) + (g0 + 2 * JOB_G), f + tail_uses(n0))
                        if pos == 5:
                            hidden_lo(f + tile0, f)
                per_job = tiles * F_CHUNKS // 2
                g1, n1 = g0 + tiles * 2 * JOB_G, n0 + 2 * tiles
                for pos in range(4 * per_job):
                    split_lo(g1 + pos)
                    if pos == 2:
                        hidden(g1, tail_uses(n1 - 2))
                    if pos == 5:
                        hidden_lo(tile0 + tiles - 1, tiles - 1)
                    for m in range(3):
                        if pos == (m + 1) * per_job + 2:
                            down(i, m, g1 + (m + 1) * per_job)
            down(2, 3, G_END)
            dve.wait_ge(y_squared, 4)
            nc.vector.tensor_reduce(ssq, ssq_n, AX.X, ALU.add).then_inc(squares_ready, 1)
            dve.wait_ge(rstd_ready, NORM_Y)
            dve.wait_ge(yg_ready, 8)
            for n in range(4):
                for t in range(TT):
                    cols = slice(n * NT, (n + 1) * NT)
                    nc.vector.scalar_tensor_tensor(res[:, t, cols], yg[:, t, cols], rstd_n[:, t:t + 1],
                                                   res[:, t, cols], ALU.mult, ALU.add).then_inc(out_ready, 1)

        @block.gpsimd
        def _(pool):
            nc.gpsimd.memset(rel_sb[REL_BUCKETS:REL_BUCKETS + 1, :], 1.0).then_inc(rel_ones_set, 1)
            pool.wait_ge(rel_ones_set, 1)
            nc.gpsimd.memset(ones[:, :], 1.0)
            nc.gpsimd.memset(eps_col, EPS).then_inc(consts_set, 1)
            with pool.Fori(0, HEADS) as h:
                pool.wait_ge(b_ready, h + 1)
                for l in range(LEVELS):
                    m = 1 << l
                    halves = decay[:, l, :].rearrange("p (n x m) -> p n x m", x=2, m=m)
                    b_halves = b.rearrange("p (n x m) -> p n x m", x=2, m=m)
                    ref = b_halves[:, :, 0, m - 1:m].to_broadcast((P, SEQ // (2 * m), m))
                    nc.gpsimd.tensor_tensor(halves[:, :, 0, :], ref, b_halves[:, :, 0, :], ALU.subtract)
                    nc.gpsimd.tensor_tensor(halves[:, :, 1, :], b_halves[:, :, 1, :], ref,
                                            ALU.subtract).then_inc(decay_log, 1)
                nc.gpsimd.tensor_tensor(decay[:, LEVELS, 0:P], b[:, P - 1:P].to_broadcast((P, P)), b[:, 0:P],
                                        ALU.subtract)
                nc.gpsimd.tensor_copy(decay[:, LEVELS, P:SEQ], b[:, P:SEQ]).then_inc(decay_log, 1)


def _granules(w, width):
    rows, cols = w.shape
    return np.ascontiguousarray(w.reshape(rows // (2 * P), 2, P, cols // width, width).transpose(3, 0, 2, 1, 4)
                                ).reshape(cols // width, rows // (2 * P), P, 2 * width)


def _distance_table():
    exact = REL_BUCKETS // 2
    table = np.zeros((REL_BUCKETS + 1, BETA), np.float32)
    for i in range(BETA):
        d = SEQ - 1 - i
        count = sum(d % dilation == 0 and d <= window for window, dilation in BRANCHES) if d >= 0 else 0
        if d >= 0:
            bucket = d if d < exact else min(REL_BUCKETS - 1, exact + int(
                np.float32(math.log(d / exact) / math.log(REL_MAX_DIST / exact) * (REL_BUCKETS - exact))))
            table[bucket, i] = 1.0
        table[REL_BUCKETS, i] = math.log(count) if count else MASKED
    return table


def _level_masks():
    s, t = np.arange(P)[:, None], np.arange(P)[None, :]
    return np.stack([((s >> (l + 1)) == (t >> (l + 1))) & ((s >> l) % 2 == 0) & ((t >> l) % 2 == 1)
                     for l in range(LEVELS)], axis=1).astype(np.int32)


def kernel(x, mem, rel_bias, lb_logits, norm_gains, w_in, hg_norm, w_out, w_cq, w_ckv, w_co, w_gate_up, w_down):
    import concourse.bacc as bacc
    from concourse.bass_utils import run_bass_kernel_spmd

    a = {k: np.asarray(v) for k, v in dict(
        x=x, mem=mem, rel_bias=rel_bias, gains=norm_gains, w_in=w_in, hg_norm=hg_norm, w_out=w_out, w_cq=w_cq,
        w_ckv=w_ckv, w_co=w_co, w_gate_up=w_gate_up, w_down=w_down).items()}
    gains = a["gains"][0]
    by_head = a["w_in"][0].reshape(D, 7, HEADS, DH)
    in_a = by_head[:, 0:4].transpose(0, 2, 1, 3).reshape(D, HEADS * NT)
    in_b = by_head[:, 4:7].transpose(0, 2, 1, 3).reshape(D, HEADS * NB)
    mix_order = [*range(7), *range(8, 15), 7, 15]
    out_w = a["w_out"][0].reshape(DC, P, D)[mix_order].reshape(D, D)
    gate, up = _granules(a["w_gate_up"][0][:, :D_FF], NT), _granules(a["w_gate_up"][0][:, D_FF:], NT)
    cols = lambda g: g.reshape(DC, P).T
    arrays = {
        "x": a["x"][0],
        "xt": np.ascontiguousarray(a["x"][0].T),
        "mem": a["mem"][0],
        "memt": np.ascontiguousarray(a["mem"][0].T),
        "rel_bias": a["rel_bias"],
        "ident": np.eye(P, dtype=np.float32),
        "flip": np.ascontiguousarray(np.eye(P, dtype=np.float32)[::-1]),
        "masks": _level_masks(),
        "onehot": _distance_table(),
        "gain_cols": np.ascontiguousarray(np.stack([cols(gains[i]) for i in (0, 3, 2, 5)], axis=1)),
        "gain_rows": np.ascontiguousarray(gains[[1, 4, 6]]),
        "hg_gain": np.ascontiguousarray(a["hg_norm"][0].reshape(HEADS, DH).T),
        "w_in_a": _granules(in_a, NT),
        "w_in_b": _granules(in_b, NB),
        "w_ckv": _granules(a["w_ckv"][0], NT),
        "w_out": _granules(out_w, NT),
        "w_cq": _granules(a["w_cq"][0], NT),
        "w_co": _granules(a["w_co"][0], NT),
        "w_gate_up": np.ascontiguousarray(np.stack([gate, up], axis=1)),
        "w_down": _granules(a["w_down"][0], NT),
    }
    nc = bacc.Bacc("TRN2", target_bir_lowering=False, num_devices=1)
    args, maps = [], {}
    for name, value in arrays.items():
        maps[f"in_{name}"] = value
        args.append(nc.dram_tensor(f"in_{name}", value.shape, mybir.dt.from_np(value.dtype), kind="ExternalInput").ap())
    beta = nc.dram_tensor("beta", (HEADS, BETA), F32, kind="Internal").ap()
    out = nc.dram_tensor("out_0", (SEQ, D), F32, kind="ExternalOutput").ap()
    layer_kernel(nc, *args, beta, out)
    result = run_bass_kernel_spmd(nc, [maps], core_ids=[0])
    return result.results[0]["out_0"].reshape(1, SEQ, D)
```

```python
import math
from contextlib import ExitStack

import numpy as np

import concourse.bass as bass
from concourse import mybir

F32 = mybir.dt.float32
F32R = mybir.dt.float32r
BF16 = mybir.dt.bfloat16
U8 = mybir.dt.uint8
I32 = mybir.dt.int32
ALU = mybir.AluOpType
ACT = mybir.ActivationFunctionType
AX = mybir.AxisListType

P = 128
D = 2048
SEQ = 256
TT = SEQ // P
DC = D // P
HEADS = 8
DH = 128
CROSS_HEADS = 4
CROSS_DH = D // CROSS_HEADS
CC = CROSS_DH // P
D_FF = 5632
NT = 512
NB = 384
F_CHUNKS = NT // P
GROUP_TILES = (4, 4, 3)
REL_BUCKETS = 32
REL_MAX_DIST = 2048
BRANCHES = ((128, 1), (512, 4), (2048, 16))
EPS = 1e-6
MASKED = -1e30
LEVELS = 7
BETA = 384
RING = 4
JOB_G = DC // 2
BODY_G = 3 * JOB_G
G_BODY = 2 * JOB_G
G_LAST_HEAD = G_BODY + (HEADS - 1) * BODY_G
G_OUT = G_LAST_HEAD + JOB_G
G_CQ = G_OUT + 4 * JOB_G
G_CO = G_CQ + 4 * JOB_G
G_FFN = G_CO + 4 * JOB_G
DMA = 16


def layer_kernel(nc, x, xt, memt, rel_bias, ident_in, flip_in, masks_in, onehot_in, gain_cols_in,
                 gain_rows_in, hg_gain_in, w_in_a, w_in_b, w_ckv, w_out, w_cq, w_co, w_gate_up,
                 w_down, beta_dram, out):
    ctx = ExitStack()
    with ctx:
        def sb(name, shape, dt=F32):
            return ctx.enter_context(nc.sbuf_tensor(name, shape, dt))

        def psum(name):
            return ctx.enter_context(nc.psum_tensor(name, [P, 512], F32))

        def sem(name):
            return ctx.enter_context(nc.semaphore(name))

        raw = sb("raw", [P, RING, 2 * NT])
        w_hi = sb("w_hi", [P, RING, 2 * NT], F32R)
        w_lo = sb("w_lo", [P, RING, 2 * NT], F32R)
        a_hi = sb("a_hi", [P, DC, SEQ], F32R)
        a_lo = sb("a_lo", [P, DC, SEQ], F32R)
        b_hi = sb("b_hi", [P, DC, SEQ], F32R)
        b_lo = sb("b_lo", [P, DC, SEQ], F32R)
        r1 = sb("r1", [P, 2 * D])
        r2 = sb("r2", [P, 2 * D])
        r3 = sb("r3", [P, 4 * D])
        r4 = sb("r4", [P, D])
        work = sb("work", [P, 4096])
        ident = sb("ident", [P, P])
        ones = sb("ones", [P, P])
        masks = sb("masks", [P, LEVELS, P], U8)
        gcol = sb("gcol", [P, 4, DC])
        hg_gain = sb("hg_gain", [P, HEADS])
        eps_col = sb("eps_col", [P, 1])[:, :]
        junk = sb("junk", [P, 4, NT], BF16)
        stat = sb("stat", [P, 64])

        mix_t = r1[:, :].rearrange("p (c s) -> p c s", c=DC)
        sub = r1[:, :].rearrange("p (t d) -> p t d", t=TT)
        res = r2[:, :].rearrange("p (t d) -> p t d", t=TT)
        decay = r2[:, 0:2048].rearrange("p (l s) -> p l s", l=LEVELS + 1)
        proj_a = r2[:, 2048:3072].rearrange("p (t n) -> p t n", t=TT)
        proj_b = r2[:, 3072:3840].rearrange("p (t n) -> p t n", t=TT)
        x_t = r3[:, 0:4096].rearrange("p (c s) -> p c s", c=DC)
        mem_t = r3[:, 4096:8192].rearrange("p (c s) -> p c s", c=DC)
        ckv = r3[:, :].rearrange("p (t n) -> p t n", t=TT)
        gs = r3[:, 1024:2048].rearrange("p (t n) -> p t n", t=TT)
        hid = r3[:, 2048:3072].rearrange("p (t n) -> p t n", t=TT)
        yg = r3[:, 4096:8192].rearrange("p (t d) -> p t d", t=TT)
        bias_rev = r1[:, 0:HEADS * SEQ].rearrange("p (h j) -> p h j", h=HEADS)
        bias = r4[:, :].rearrange("p (h j) -> p h j", h=HEADS)
        x_squares, x_sum, mem_sum = r1[:, 2048:2560], r1[:, 2560:3072], r1[:, 3072:3584]
        mem_squares = r2[:, 0:2048].rearrange("p (i n) -> p i n", i=4)
        gain_row = r4
        qk_t = work[:, 0:512]
        sig = work[:, 512:1024]
        qg = work[:, 1024:1280]
        kk = work[:, 1280:1536]
        logf = work[:, 1536:1792]
        b = work[:, 1792:2048]
        att = work[:, 2048:2304]
        att_x = work[:, 2304:2432]
        prob = work[:, 2432:2816]
        prob_t = work[:, 2816:3200]
        gsil = work[:, 3200:3456].rearrange("p (t n) -> p t n", t=TT)
        y_hg = work[:, 3456:3712].rearrange("p (t n) -> p t n", t=TT)
        onehot = work[0:REL_BUCKETS + 1, 0:BETA]
        rel_sb = work[0:REL_BUCKETS + 1, BETA:BETA + HEADS]
        flip = work[:, 1024:1024 + P]
        masks_wide = work[:, 1152:1152 + LEVELS * P].bitcast(I32).rearrange("p (l n) -> p l n", l=LEVELS)
        beta_sb = work[0:HEADS, 512:512 + BETA]
        cq = work[:, 0:1024].rearrange("p (t n) -> p t n", t=TT)
        cq_t = work[:, 1024:2048].rearrange("p (c s) -> p c s", c=CC)
        ck_t = work[:, 2048:3072].rearrange("p (c s) -> p c s", c=CC)
        cprob = work[:, 3072:3584].rearrange("p (t m) -> p t m", t=TT)
        cprob_t = work[:, 3584:4096].rearrange("p (m s) -> p m s", m=TT)
        ssq = stat[:, 0:2]
        rstd_x = stat[:, 2:4]
        rstd_m = stat[:, 6:8]
        neg_max = stat[:, 8:10]
        row_sum = stat[:, 10:12]
        ssq_o = stat[:, 12:14]
        rstd_o = stat[:, 14:16]
        ssq_n = stat[:, 16:24].rearrange("p (t n) -> p t n", t=TT)
        rstd_n = stat[:, 24:26]
        ssq_r = stat[:, 26:34].rearrange("p (t n) -> p t n", t=TT)
        rstd_r = stat[:, 34:36]

        OUT_VECTOR, OUT_POOL = [(0, 0), (0, 1), (1, 0), (1, 1), (2, 0), (2, 1)], [(3, 0), (3, 1)]
        TURN_AT = (0, 0, 3, 5)

        acc = [[psum("acc00"), psum("acc01")], [psum("acc10"), psum("acc11")]]
        s0, s1, s2, s3 = psum("s0"), psum("s1"), psum("s2"), psum("s3")
        small = [s0, s1, s2, s3]

        raw_landed = [sem(f"raw_landed{i}") for i in range(RING)]
        hi_ready, lo_ready, granule_used = sem("hi_ready"), sem("lo_ready"), sem("granule_used")
        acc_free = [sem("acc_free0"), sem("acc_free1")]
        xt_landed = [sem(f"xt_landed{i}") for i in range(JOB_G)]
        gcol_landed, rel_landed, ident_landed, const_landed = (
            sem("gcol_landed"), sem("rel_landed"), sem("ident_landed"), sem("const_landed"))
        memt_landed = [sem(f"memt_landed{i}") for i in range(JOB_G)]
        masks_ready = sem("masks_ready")
        consts_set, rel_ones_set = sem("consts_set"), sem("rel_ones_set")
        beta_done, beta_stored, bias_landed, flip_done, bias_ready = (
            sem("beta_done"), sem("beta_stored"), sem("bias_landed"), sem("flip_done"), sem("bias_ready"))
        a_hi_ready, a_lo_ready, b_hi_ready, b_lo_ready = (
            sem("a_hi_ready"), sem("a_lo_ready"), sem("b_hi_ready"), sem("b_lo_ready"))
        x_squared, x_summed, mem_squared, mem_summed = (
            sem("x_squared"), sem("x_summed"), sem("mem_squared"), sem("mem_summed"))
        squares_ready, log_ready, rstd_ready = sem("squares_ready"), sem("log_ready"), sem("rstd_ready")
        qk_turned, fz_turned, qk_copied = sem("qk_turned"), sem("fz_turned"), sem("qk_copied")
        sig_ready, qg_ready, kk_ready = sem("sig_ready"), sem("qg_ready"), sem("kk_ready")
        logf_ready, b_ready, decay_log, decay_ready, factors_ready = (
            sem("logf_ready"), sem("b_ready"), sem("decay_log"), sem("decay_ready"), sem("factors_ready"))
        level_done, level_merged, cross_done, cross_copied = (
            sem("level_done"), sem("level_merged"), sem("cross_done"), sem("cross_copied"))
        o_done, o_squared, o_log, o_rstd, y_ready, y_turned = (
            sem("o_done"), sem("o_squared"), sem("o_log"), sem("o_rstd"), sem("y_ready"), sem("y_turned"))
        gz_sig, gz_silu = sem("gz_sig"), sem("gz_silu")
        scores_done, logits_ready, max_ready, prob_exp, sum_inv = (
            sem("scores_done"), sem("logits_ready"), sem("max_ready"), sem("prob_exp"), sem("sum_inv"))
        prob_ready, prob_turned, prob_t_ready, pv_done, attn_copied = (
            sem("prob_ready"), sem("prob_turned"), sem("prob_t_ready"), sem("pv_done"), sem("attn_copied"))
        s3_copied = sem("s3_copied")
        gain_landed, res_landed = sem("gain_landed"), sem("res_landed")
        sub0_scaled, sub1_squared, res_ready, res_turned, res_squared = (
            sem("sub0_scaled"), sem("sub1_squared"), sem("res_ready"), sem("res_turned"), sem("res_squared"))
        cqk_turned, cqk_t_ready, cscores_done, cmax_ready, cbias_ready, cprob_exp, csum_inv = (
            sem("cqk_turned"), sem("cqk_t_ready"), sem("cscores_done"), sem("cmax_ready"), sem("cbias_ready"),
            sem("cprob_exp"), sem("csum_inv"))
        cprob_ready, cprob_turned, cprob_t_ready, cpv_done = (
            sem("cprob_ready"), sem("cprob_turned"), sem("cprob_t_ready"), sem("cpv_done"))
        hid_turned, y_scaled = sem("hid_turned"), sem("y_scaled")
        y_squared, yg_ready, out_ready, out_ready_pool, out_stored = (
            sem("y_squared"), sem("yg_ready"), sem("out_ready"), sem("out_ready_pool"), sem("out_stored"))

        def attn_chunk(h):
            return 14 if isinstance(h, int) and h == HEADS - 1 else h

        def hg_chunk(h):
            return 15 if isinstance(h, int) and h == HEADS - 1 else h + 7

        def tail_pair(n):
            return (n + 1) % 2

        def tail_uses(n):
            return n // 2 + (HEADS if n % 2 == 0 else 2 * HEADS)

        JOB_FFN = 12

        groups, tile0, g0, j0 = [], 0, G_FFN, JOB_FFN
        for tiles in GROUP_TILES:
            groups.append((tile0, tiles, g0, j0))
            tile0 += tiles
            g0 += tiles * 2 * JOB_G + 4 * tiles * F_CHUNKS // 2
            j0 += tiles * 2 + 4
        G_END = g0

        A_PIECES = DC + 4

        NORM_X, NORM_MEM, NORM_OUT, NORM_CQ = range(1, 5)
        NORM_Y = 7

        block = ctx.enter_context(nc.Block())

        @block.sync
        def _(sp):
            def load(g, source, width, it=0, per=0):
                if g >= RING:
                    sp.wait_ge(lo_ready, it * per + (g - RING + 1))
                sp.dma_start(raw[:, g % RING, 0:width], source).then_inc(raw_landed[g % RING], DMA)

            def load_job(g, source, width, it=0, per=0):
                for j in range(JOB_G):
                    load(g + j, source[j], width, it, per)

            xt_v = xt.rearrange("(q c p) s -> q p c s", q=JOB_G, p=P)
            for j in range(JOB_G):
                sp.dma_start(x_t[:, 2 * j:2 * j + 2, :], xt_v[j]).then_inc(xt_landed[j], DMA)
                load(j, w_in_a[0, j], 2 * NT)
            memt_v = memt.rearrange("(q c p) s -> q p c s", q=JOB_G, p=P)
            for j in range(JOB_G):
                sp.dma_start(mem_t[:, 2 * j:2 * j + 2, :], memt_v[j]).then_inc(memt_landed[j], DMA)
                load(JOB_G + j, w_in_b[0, j], 2 * NB)
            with sp.Fori(0, HEADS - 1) as h:
                for j in range(JOB_G):
                    load(G_BODY + j, w_ckv[h, j], 2 * NT, h, BODY_G)
                for j in range(JOB_G):
                    load(G_BODY + JOB_G + j, w_in_a[h + 1, j], 2 * NT, h, BODY_G)
                for j in range(JOB_G):
                    load(G_BODY + 2 * JOB_G + j, w_in_b[h + 1, j], 2 * NB, h, BODY_G)
            load_job(G_LAST_HEAD, w_ckv[HEADS - 1], 2 * NT)
            for n in range(4):
                if n == 2:
                    sp.wait_ge(y_turned, HEADS)
                    sp.wait_ge(gz_silu, HEADS)
                    sp.dma_start(res, x.rearrange("(t p) d -> p t d", p=P)).then_inc(res_landed, DMA)
                if n == 1:
                    sp.wait_ge(logits_ready, HEADS)
                    sp.dma_start(gain_row[:, :], gain_rows_in[0:1, :].to_broadcast((P, D))).then_inc(gain_landed, DMA)
                load_job(G_OUT + n * JOB_G, w_out[n], 2 * NT)
            for n in range(4):
                load_job(G_CQ + n * JOB_G, w_cq[n], 2 * NT)
            sp.wait_ge(res_ready, 8)
            sp.dma_start(gain_row[:, :], gain_rows_in[1:2, :].to_broadcast((P, D))).then_inc(gain_landed, DMA)
            for n in range(4):
                load_job(G_CO + n * JOB_G, w_co[n], 2 * NT)
            for n, (tile0, tiles, g0, _) in enumerate(groups):
                for job in range(2):
                    load_job(g0 + job * JOB_G, w_gate_up[tile0, job], 2 * NT)
                if n == 0:
                    sp.wait_ge(res_ready, 16)
                    sp.dma_start(gain_row[:, :], gain_rows_in[2:3, :].to_broadcast((P, D))).then_inc(gain_landed, DMA)
                with sp.Fori(0, tiles - 1) as f:
                    for job in range(2):
                        for j in range(JOB_G):
                            load(g0 + (2 + job) * JOB_G + j, w_gate_up[f + (tile0 + 1), job, j], 2 * NT, f, 2 * JOB_G)
                g, k0, per_job = g0 + tiles * 2 * JOB_G, tile0 * F_CHUNKS // 2, tiles * F_CHUNKS // 2
                for job in range(4):
                    for j in range(per_job):
                        load(g + job * per_job + j, w_down[job, k0 + j], 2 * NT)
            for n, t in (*OUT_VECTOR[:3], OUT_POOL[0], *OUT_VECTOR[3:5], OUT_POOL[1], *OUT_VECTOR[5:]):
                if (n, t) in OUT_VECTOR:
                    sp.wait_ge(out_ready, OUT_VECTOR.index((n, t)) + 1)
                else:
                    sp.wait_ge(out_ready_pool, OUT_POOL.index((n, t)) + 1)
                sp.dma_start(out[t * P:(t + 1) * P, n * NT:(n + 1) * NT],
                             res[:, t, n * NT:(n + 1) * NT]).then_inc(out_stored, DMA)
            sp.wait_ge(out_stored, 4 * TT * DMA)

        @block.tensor
        def _(pe):
            def use_granule(g, width, pair, hi, lo, chunk, first, last, it=0, per=0):
                slot = g % RING
                pe.wait_ge(lo_ready, it * per + (g + 1))
                for c in range(2):
                    cols = slice(c * width, (c + 1) * width)
                    for t in range(TT):
                        tile = acc[pair][t][:, 0:width]
                        x_hi = hi[:, chunk + c, t * P:(t + 1) * P]
                        x_lo = lo[:, chunk + c, t * P:(t + 1) * P]
                        nc.tensor.matmul(tile, x_hi, w_hi[:, slot, cols], start=first and c == 0, stop=False)
                        nc.tensor.matmul(tile, x_hi, w_lo[:, slot, cols], start=False, stop=False)
                        mm = nc.tensor.matmul(tile, x_lo, w_hi[:, slot, cols], start=False, stop=last and c == 1)
                mm.then_inc(granule_used, 1)

            def turn(bank, col, source):
                return nc.tensor.transpose(bank[:, col:col + P], source, ident[:, :])

            def level(bank, col, left, right):
                for t in range(TT):
                    ts = slice(t * P, (t + 1) * P)
                    mm = nc.tensor.matmul(bank[:, col + t * P:col + (t + 1) * P], left[:, ts], right[:, ts],
                                          start=True, stop=True)
                mm.then_inc(level_done, 1)

            def head_steps(pos, h):
                if pos == 0:
                    pe.wait_ge(acc_free[0], h * 4 + 2)
                    pe.wait_ge(acc_free[1], h * 2 + 2)
                    for i in range(2):
                        for t in range(TT):
                            mm = turn(s0, (2 * i + t) * P, proj_a[:, t, i * DH:(i + 1) * DH])
                    mm.then_inc(qk_turned, 1)
                    for t in range(TT):
                        turn(s1, t * P, proj_a[:, t, 3 * DH:4 * DH])
                    for t in range(TT):
                        mm = turn(s1, (2 + t) * P, proj_b[:, t, DH:2 * DH])
                    mm.then_inc(fz_turned, 1)
                if pos == 2:
                    pe.wait_ge(qk_copied, h + 1)
                    nc.tensor.matmul(s2[:, 0:SEQ], qk_t[:, P:2 * P], qk_t[:, 2 * P:4 * P], start=True, stop=True)
                    nc.tensor.matmul(s2[:, SEQ:SEQ + P], qk_t[:, 0:P], qk_t[:, 2 * P:3 * P],
                                     start=True, stop=True).then_inc(scores_done, 1)
                if pos == 5:
                    pe.wait_ge(prob_ready, h * 2 + 2)
                    pe.wait_ge(s3_copied, h + 1)
                    turn(s3, 0, prob[:, SEQ:SEQ + P])
                    turn(s3, P, prob[:, 0:P])
                    turn(s3, 2 * P, prob[:, P:2 * P]).then_inc(prob_turned, 1)
                if pos == 6:
                    pe.wait_ge(prob_t_ready, h + 1)
                    nc.tensor.matmul(s2[:, 0:SEQ], proj_a[:, 0, 2 * DH:3 * DH], prob_t[:, 0:SEQ],
                                     start=True, stop=False)
                    nc.tensor.matmul(s2[:, P:SEQ], proj_a[:, 1, 2 * DH:3 * DH], prob_t[:, SEQ:SEQ + P],
                                     start=False, stop=True).then_inc(pv_done, 1)
                if pos == 7:
                    pe.wait_ge(kk_ready, h + 1)
                    pe.wait_ge(qg_ready, h + 1)
                    level(s0, 0, kk, qg)
                    pe.wait_ge(factors_ready, h * 8 + 1)
                    level(s0, SEQ, decay[:, 0, :], decay[:, 0, :])
                if pos == 8:
                    for l, bank, col in ((1, s1, 0), (2, s1, SEQ), (3, s3, 0), (4, s3, SEQ)):
                        pe.wait_ge(factors_ready, h * 8 + (l + 1))
                        level(bank, col, decay[:, l, :], decay[:, l, :])
                if pos == 9:
                    pe.wait_ge(level_merged, h * 8 + 2)
                    for l, col in ((5, 0), (6, SEQ)):
                        pe.wait_ge(factors_ready, h * 8 + (l + 1))
                        level(s0, col, decay[:, l, :], decay[:, l, :])
                    pe.wait_ge(level_merged, h * 8 + 4)
                    pe.wait_ge(factors_ready, h * 8 + 8)
                    nc.tensor.matmul(s1[:, 0:P], decay[:, LEVELS, 0:P], decay[:, LEVELS, P:SEQ],
                                     start=True, stop=True).then_inc(cross_done, 1)
                if pos == 11:
                    pe.wait_ge(level_merged, h * 8 + 8)
                    pe.wait_ge(cross_copied, h + 1)
                    pe.wait_ge(attn_copied, h + 1)
                    nc.tensor.matmul(s2[:, 0:DH], att[:, 0:P], proj_b[:, 0, 0:DH], start=True, stop=True)
                    nc.tensor.matmul(s2[:, DH:2 * DH], att_x, proj_b[:, 0, 0:DH], start=True, stop=False)
                    nc.tensor.matmul(s2[:, DH:2 * DH], att[:, P:SEQ], proj_b[:, 1, 0:DH],
                                     start=False, stop=True).then_inc(o_done, 1)
                if pos == 13:
                    pe.wait_ge(y_ready, h + 1)
                    turn(s3, 0, y_hg[:, 0, :])
                    turn(s3, P, y_hg[:, 1, :]).then_inc(y_turned, 1)

            def turn_residual(k, n):
                if k == 0 and n == 0:
                    pe.wait_ge(s3_copied, HEADS + 1)
                if n >= 2:
                    pe.wait_ge(a_lo_ready, A_PIECES + DC * k + 4 * (n - 1))
                for i in range(2):
                    for t in range(TT):
                        pe.wait_ge(res_ready, 8 * k + 2 * n + t + 1)
                        for c in range(2):
                            chunk = 4 * n + 2 * i + c
                            mm = turn(small[(2 * n + i) % 4], (2 * c + t) * P, res[:, t, chunk * P:(chunk + 1) * P])
                    mm.then_inc(res_turned, 1)

            def residual_operand(k, j):
                for n in range(4):
                    if TURN_AT[n] == j:
                        turn_residual(k, n)
                pe.wait_ge(a_lo_ready, A_PIECES + DC * k + 2 * j + 2)

            def cross_steps(pos, j):
                if pos == 0:
                    n = 4 + j
                    pe.wait_ge(acc_free[tail_pair(n)], 2 * tail_uses(n) + 2)
                    if j > 0:
                        pe.wait_ge(b_lo_ready, DC + 2 * j)
                    for i in range(2):
                        for c in range(2):
                            for t in range(TT):
                                chunk = 2 * i + c
                                mm = turn(small[i], (2 * c + t) * P, cq[:, t, chunk * P:(chunk + 1) * P])
                        mm.then_inc(cqk_turned, 1)
                    for i in range(2):
                        for c in range(2):
                            for m in range(TT):
                                col = j * CROSS_DH + (2 * i + c) * P
                                mm = turn(small[2 + i], (2 * c + m) * P, ckv[:, m, col:col + P])
                        mm.then_inc(cqk_turned, 1)
                if pos == 1:
                    pe.wait_ge(cqk_t_ready, 4 * j + 4)
                    for t in range(TT):
                        for c in range(CC):
                            mm = nc.tensor.matmul(s0[:, t * SEQ:(t + 1) * SEQ], cq_t[:, c, t * P:(t + 1) * P],
                                                  ck_t[:, c, :], start=c == 0, stop=c == CC - 1)
                    mm.then_inc(cscores_done, 1)
                if pos == 3:
                    pe.wait_ge(cprob_ready, j + 1)
                    for m in range(TT):
                        for t in range(TT):
                            mm = turn(s1, (2 * m + t) * P, cprob[:, t, m * P:(m + 1) * P])
                    mm.then_inc(cprob_turned, 1)
                if pos == 4:
                    pe.wait_ge(cprob_t_ready, j + 1)
                    for c in range(CC):
                        col = D + j * CROSS_DH + c * P
                        for m in range(TT):
                            mm = nc.tensor.matmul(small[2 + c // 2][:, (c % 2) * SEQ:(c % 2 + 1) * SEQ],
                                                  ckv[:, m, col:col + P], cprob_t[:, m, :], start=m == 0, stop=m == 1)
                        if c % 2:
                            mm.then_inc(cpv_done, 1)

            def turn_hidden(tile, uses):
                pe.wait_ge(acc_free[0], uses * 2 + 2)
                pe.wait_ge(b_lo_ready, tile * 2 + (DC + 8))
                for i in range(2):
                    for c in range(2):
                        for t in range(TT):
                            mm = turn(small[i], (2 * c + t) * P, hid[:, t, (2 * i + c) * P:(2 * i + c + 1) * P])
                    mm.then_inc(hid_turned, 1)

            def sum_features(bank, squares):
                for t in range(TT):
                    for c in range(2):
                        mm = nc.tensor.matmul(bank[:, t:t + 1], squares[:, c * SEQ + t * P:c * SEQ + (t + 1) * P],
                                              ones[:, 0:1], start=c == 0, stop=c == 1)
                mm.then_inc(squares_ready, 1)

            for j in range(JOB_G):
                pe.wait_ge(a_lo_ready, 2 * j + 2)
                use_granule(j, NT, 0, a_hi, a_lo, 2 * j, j == 0, j == JOB_G - 1)
                if j == 0:
                    pe.wait_ge(rel_landed, 2 * DMA)
                    pe.wait_ge(rel_ones_set, 1)
                    nc.tensor.matmul(s3[0:HEADS, 0:BETA], rel_sb, onehot, start=True, stop=True).then_inc(beta_done, 1)
                if j == 7:
                    pe.wait_ge(ident_landed, 2 * DMA)
                    pe.wait_ge(bias_landed, DMA)
                    pe.wait_ge(s3_copied, 1)
                    for i in range(4):
                        nc.tensor.matmul(small[i][:, :], flip, r1[:, i * 512:(i + 1) * 512],
                                         start=True, stop=True).then_inc(flip_done, 1)
            pe.wait_ge(consts_set, 1)
            for j in range(JOB_G):
                use_granule(JOB_G + j, NB, 1, a_hi, a_lo, 2 * j, j == 0, j == JOB_G - 1)
                if j == 1:
                    pe.wait_ge(x_summed, JOB_G)
                    pe.wait_ge(bias_ready, 4)
                    sum_features(s1, x_sum)
                if j == 5:
                    pe.wait_ge(mem_summed, JOB_G - 1)
                    sum_features(s2, mem_sum)
            pe.wait_ge(b_lo_ready, DC)

            with pe.Fori(0, HEADS - 1) as h:
                pe.wait_ge(acc_free[0], h * 4 + 2)
                for j in range(JOB_G):
                    use_granule(G_BODY + j, NT, 0, b_hi, b_lo, 2 * j, j == 0, j == JOB_G - 1, h, BODY_G)
                    head_steps(j, h)
                pe.wait_ge(acc_free[0], h * 4 + 4)
                for j in range(JOB_G):
                    use_granule(G_BODY + JOB_G + j, NT, 0, a_hi, a_lo, 2 * j, j == 0, j == JOB_G - 1, h, BODY_G)
                    head_steps(JOB_G + j, h)
                pe.wait_ge(acc_free[1], h * 2 + 2)
                for j in range(JOB_G):
                    use_granule(G_BODY + 2 * JOB_G + j, NB, 1, a_hi, a_lo, 2 * j, j == 0, j == JOB_G - 1, h, BODY_G)

            last = HEADS - 1
            pe.wait_ge(acc_free[0], last * 4 + 2)
            for j in range(JOB_G):
                use_granule(G_LAST_HEAD + j, NT, 0, b_hi, b_lo, 2 * j, j == 0, j == JOB_G - 1)
                head_steps(j, last)

            def tail_job(n, g, granules, hi, lo, before=None, after=None):
                pe.wait_ge(acc_free[tail_pair(n)], 2 * tail_uses(n))
                for j in range(granules):
                    if before:
                        before(j)
                    use_granule(g + j, NT, tail_pair(n), hi, lo, 2 * j, j == 0, j == granules - 1)
                    if after:
                        after(j)

            def mix_split(j):
                pe.wait_ge(a_lo_ready, 17 if j < 3 else 18 if j < 7 else 20)

            tail_job(0, G_OUT, JOB_G, a_hi, a_lo, mix_split, lambda j: head_steps(JOB_G + j, last))
            for n in range(1, 4):
                tail_job(n, G_OUT + n * JOB_G, JOB_G, a_hi, a_lo)
            for j in range(CROSS_HEADS):
                tail_job(4 + j, G_CQ + j * JOB_G, JOB_G, a_hi, a_lo,
                         None if j else (lambda k: residual_operand(0, k)),
                         (lambda k: cross_steps(k, j - 1)) if j else None)
            tail_job(8, G_CO, JOB_G, b_hi, b_lo, lambda k: pe.wait_ge(b_lo_ready, DC + k + 1),
                     lambda k: cross_steps(k, CROSS_HEADS - 1))
            for n in range(1, 4):
                tail_job(8 + n, G_CO + n * JOB_G, JOB_G, b_hi, b_lo)
            for tile0, tiles, g0, n0 in groups:
                tail_job(n0, g0, JOB_G, a_hi, a_lo, None if tile0 else (lambda k: residual_operand(1, k)))
                tail_job(n0 + 1, g0 + JOB_G, JOB_G, a_hi, a_lo)
                with pe.Fori(0, tiles - 1) as f:
                    pe.wait_ge(acc_free[1], f * 2 + (2 * tail_uses(n0) + 2))
                    for j in range(JOB_G):
                        use_granule(g0 + 2 * JOB_G + j, NT, 1, a_hi, a_lo, 2 * j, j == 0, j == JOB_G - 1, f, 2 * JOB_G)
                        if j == 1:
                            turn_hidden(f + tile0, f + tail_uses(n0 + 1))
                    pe.wait_ge(acc_free[0], f * 2 + (2 * tail_uses(n0 + 1) + 2))
                    for j in range(JOB_G):
                        use_granule(g0 + 3 * JOB_G + j, NT, 0, a_hi, a_lo, 2 * j, j == 0, j == JOB_G - 1, f, 2 * JOB_G)
                per_job = tiles * F_CHUNKS // 2
                g1, n1 = g0 + tiles * 2 * JOB_G, n0 + 2 * tiles
                for m in range(4):
                    tail_job(n1 + m, g1 + m * per_job, per_job, b_hi, b_lo,
                             (lambda k: pe.wait_ge(b_lo_ready, DC + 8 + 2 * tile0 + k + 1)) if m == 0 else None,
                             (lambda k: turn_hidden(tile0 + tiles - 1, tail_uses(n1 - 1)) if k == 1 else None)
                             if m == 0 else None)

        @block.scalar
        def _(act):
            def split_hi(g, width=2 * NT, it=0, per=0):
                slot = g % RING
                act.wait_ge(raw_landed[slot], it * (per // RING * DMA) + (g // RING + 1) * DMA)
                if g >= RING:
                    act.wait_ge(granule_used, it * per + (g - RING + 1))
                nc.scalar.activation(w_hi[:, slot, 0:width], raw[:, slot, 0:width], ACT.Copy).then_inc(hi_ready, 1)

            def rstd(squares, to, count):
                act.wait_ge(squares_ready, count)
                nc.scalar.activation(to, squares, ACT.Ln, scale=1.0 / D, bias=eps_col).then_inc(log_ready, 1)
                act.wait_ge(log_ready, count)
                nc.scalar.activation(to, to, ACT.Exp, scale=-0.5).then_inc(rstd_ready, 1)

            def copy_out(used, bank, to, scale, pair):
                act.wait_ge(granule_used, used)
                nc.scalar.activation(to, bank, ACT.Copy, scale=scale).then_inc(acc_free[pair], 1)

            def head_steps(pos, h, used):
                if pos == 2:
                    copy_out(used, acc[1][0][:, 0:NB], proj_b[:, 0, :], rstd_x[:, 0:1], 1)
                if pos == 4:
                    act.wait_ge(qk_turned, h + 1)
                    nc.scalar.activation(qk_t, s0[:, :], ACT.Copy).then_inc(qk_copied, 1)
                    act.wait_ge(fz_turned, h + 1)
                    nc.scalar.activation(sig, s1[:, :], ACT.Sigmoid).then_inc(sig_ready, 1)
                    act.wait_ge(acc_free[1], h * 2 + 2)
                    nc.scalar.activation(gsil, proj_b[:, :, 2 * DH:3 * DH], ACT.Sigmoid).then_inc(gz_sig, 1)
                    nc.scalar.preload_act_table_set("natural_log_exp_and_others")
                    act.wait_ge(sig_ready, h + 1)
                    nc.scalar.activation(logf, sig[:, 0:SEQ], ACT.Ln).then_inc(logf_ready, 1)
                if pos == 6:
                    act.wait_ge(max_ready, h * 2 + 2)
                    nc.scalar.activation(prob[:, 0:SEQ], prob[:, 0:SEQ], ACT.Exp, bias=neg_max[:, 1:2],
                                         accum_out=row_sum[:, 1:2])
                    nc.scalar.activation(prob[:, SEQ:SEQ + P], prob[:, SEQ:SEQ + P], ACT.Exp, bias=neg_max[:, 0:1],
                                         accum_out=row_sum[:, 0:1]).then_inc(prob_exp, 1)
                if pos == 8:
                    act.wait_ge(decay_log, h * 8 + 4)
                    nc.scalar.activation(decay[:, 0:4, :], decay[:, 0:4, :], ACT.Exp).then_inc(decay_ready, 1)
                if pos == 9:
                    act.wait_ge(prob_turned, h + 1)
                    nc.scalar.activation(prob_t, s3[:, 0:BETA], ACT.Copy).then_inc(prob_t_ready, 1)
                    act.wait_ge(decay_log, h * 8 + 8)
                    nc.scalar.activation(decay[:, 4:8, :], decay[:, 4:8, :], ACT.Exp).then_inc(decay_ready, 1)
                if pos == 10:
                    act.wait_ge(pv_done, h + 1)
                    nc.scalar.activation(mix_t[:, attn_chunk(h), :], s2[:, 0:SEQ], ACT.Copy).then_inc(attn_copied, 1)
                    copy_out(used + JOB_G, acc[0][0][:, :], ckv[:, 0, bass.ds(h * NT, NT)], rstd_m[:, 0:1], 0)
                if pos == 13:
                    act.wait_ge(cross_done, h + 1)
                    nc.scalar.activation(att_x, s1[:, 0:P], ACT.Copy).then_inc(cross_copied, 1)
                if pos == 15:
                    act.wait_ge(o_done, h + 1)
                    nc.scalar.activation(junk[:, 0, 0:DH], s2[:, 0:DH], ACT.Square, accum_out=ssq_o[:, 0:1])
                    nc.scalar.activation(junk[:, 1, 0:DH], s2[:, DH:2 * DH], ACT.Square,
                                         accum_out=ssq_o[:, 1:2]).then_inc(o_squared, 1)
                    act.wait_ge(o_squared, h + 1)
                    nc.scalar.activation(rstd_o, ssq_o, ACT.Ln, scale=1.0 / DH, bias=eps_col).then_inc(o_log, 1)
                    act.wait_ge(o_log, h + 1)
                    nc.scalar.activation(rstd_o, rstd_o, ACT.Exp, scale=-0.5).then_inc(o_rstd, 1)
                if pos == 17:
                    act.wait_ge(y_turned, h + 1)
                    gain = hg_gain[:, h:h + 1] if isinstance(h, int) else hg_gain[:, bass.ds(h, 1)]
                    nc.scalar.activation(mix_t[:, hg_chunk(h), :], s3[:, 0:SEQ], ACT.Copy,
                                         scale=gain).then_inc(s3_copied, 1)

            def square_sub(n, m, used, k):
                pair = tail_pair(n)
                act.wait_ge(granule_used, used)
                nc.scalar.activation(junk[:, 2 * pair + 1, :], acc[pair][1][:, :], ACT.Square,
                                     accum_out=ssq_n[:, 1, m:m + 1]).then_inc(sub1_squared, 1)
                act.wait_ge(sub0_scaled, 4 * k + m + 1)
                nc.scalar.activation(junk[:, 2 * pair, :], acc[pair][0][:, :], ACT.Square,
                                     accum_out=ssq_n[:, 0, m:m + 1]).then_inc(acc_free[pair], 1)

            def operand_hi(k, n):
                for i in range(2):
                    act.wait_ge(res_turned, 8 * k + 2 * n + i + 1)
                    for c in range(2):
                        chunk = 4 * n + 2 * i + c
                        nc.scalar.activation(a_hi[:, chunk, :], small[(2 * n + i) % 4][:, c * SEQ:(c + 1) * SEQ],
                                             ACT.Copy, scale=gcol[:, 2 + k, chunk:chunk + 1]).then_inc(a_hi_ready, 1)

            def square_res(k, n):
                act.wait_ge(res_ready, 8 * k + 2 * n + 2)
                for t in range(TT):
                    done = 8 * k + 2 * n + t
                    if done >= 4:
                        act.wait_ge(res_squared, done - 3)
                    nc.scalar.activation(junk[:, done % 4, :], res[:, t, n * NT:(n + 1) * NT], ACT.Square,
                                         accum_out=ssq_r[:, t, n:n + 1]).then_inc(res_squared, 1)

            def next_operand(pos, k):
                for n in (2, 3):
                    if pos == TURN_AT[n] + 3:
                        operand_hi(k, n)
                if 5 <= pos < 9:
                    square_res(k, pos - 5)
                if pos == 9:
                    rstd(ssq, rstd_r, NORM_CQ + 2 * k)
                    act.wait_ge(rstd_ready, NORM_CQ + 2 * k)

            def cross_steps(pos, j, used):
                if pos == 2:
                    n = 4 + j
                    copy_out(used, acc[tail_pair(n)][0][:, :], cq[:, 0, :], rstd_r[:, 0:1], tail_pair(n))
                if pos == 3:
                    act.wait_ge(cqk_turned, 4 * j + 1)
                    nc.scalar.activation(cq_t[:, 0:2, :], s0[:, :], ACT.Copy).then_inc(cqk_t_ready, 1)
                    act.wait_ge(cqk_turned, 4 * j + 3)
                    nc.scalar.activation(ck_t[:, 0:2, :], s2[:, :], ACT.Copy).then_inc(cqk_t_ready, 1)
                if pos == 5:
                    act.wait_ge(cbias_ready, j + 1)
                    for t in range(TT):
                        e = nc.scalar.activation(cprob[:, t, :], s0[:, t * SEQ:(t + 1) * SEQ], ACT.Exp,
                                                 scale=CROSS_DH ** -0.5, bias=neg_max[:, t:t + 1],
                                                 accum_out=row_sum[:, t:t + 1])
                    e.then_inc(cprob_exp, 1)
                if pos == 7:
                    act.wait_ge(cprob_turned, j + 1)
                    nc.scalar.activation(cprob_t, s1[:, :], ACT.Copy).then_inc(cprob_t_ready, 1)
                if pos == 8:
                    for i in range(2):
                        act.wait_ge(cpv_done, 2 * j + i + 1)
                        nc.scalar.activation(b_hi[:, 4 * j + 2 * i:4 * j + 2 * i + 2, :], small[2 + i][:, :],
                                             ACT.Copy).then_inc(b_hi_ready, 1)

            def silu_gate(used):
                act.wait_ge(granule_used, used)
                for t in range(TT):
                    nc.scalar.activation(gs[:, t, :], acc[1][t][:, :], ACT.Silu,
                                         scale=rstd_r[:, t:t + 1]).then_inc(acc_free[1], 1)

            def hidden_hi(tile, ft):
                for i in range(2):
                    act.wait_ge(hid_turned, tile * 2 + (i + 1))
                    nc.scalar.activation(b_hi[:, bass.ds(ft * F_CHUNKS + 2 * i, 2), :], small[i][:, :],
                                         ACT.Copy).then_inc(b_hi_ready, 1)

            def act_down(i, m, used):
                n = groups[i][3] + 2 * groups[i][1] + m
                pair, cols = tail_pair(n), slice(m * NT, (m + 1) * NT)
                if i == 0:
                    copy_out(used, acc[pair][0][:, :], sub[:, 0, cols], 1.0, pair)
                if i == 2:
                    if m:
                        act.wait_ge(y_squared, m)
                    for t in range(TT):
                        act.wait_ge(acc_free[pair], 2 * tail_uses(n) + t + 1)
                        sq = nc.scalar.activation(junk[:, 2 * pair + t, :], sub[:, t, cols], ACT.Square,
                                                  accum_out=ssq_n[:, t, m:m + 1])
                    sq.then_inc(y_squared, 1)

            act.dma_start(gcol[:, :, :], gain_cols_in).then_inc(gcol_landed, DMA)
            nc.scalar.preload_act_table_set("natural_log_exp_and_others")
            act.wait_ge(gcol_landed, DMA)
            act.wait_ge(consts_set, 1)
            for pos in range(G_BODY):
                j = pos % JOB_G
                source, landed, hi, count, norm = ((x_t, xt_landed, a_hi, a_hi_ready, 0) if pos < JOB_G else
                                                   (mem_t, memt_landed, b_hi, b_hi_ready, 1))
                act.wait_ge(landed[j], DMA)
                for c in (2 * j, 2 * j + 1):
                    nc.scalar.activation(hi[:, c, :], source[:, c, :], ACT.Copy,
                                         scale=gcol[:, norm, c:c + 1]).then_inc(count, 1)
                split_hi(pos, 2 * (NT if pos < JOB_G else NB))
                if pos >= JOB_G:
                    if j > 4:
                        act.wait_ge(mem_summed, j - 4)
                    nc.scalar.activation(mem_squares[:, j % 4, :] if j else mem_sum, mem_t[:, 2 * j:2 * j + 2, :],
                                         ACT.Square).then_inc(mem_squared, 1)
                if pos == 0:
                    act.dma_start(rel_sb[0:REL_BUCKETS, :], rel_bias).then_inc(rel_landed, DMA)
                    act.dma_start(onehot, onehot_in).then_inc(rel_landed, DMA)
                if pos == 4:
                    act.wait_ge(beta_done, 1)
                    nc.scalar.activation(beta_sb, s3[0:HEADS, 0:BETA], ACT.Copy).then_inc(s3_copied, 1)
                if pos == 5:
                    act.wait_ge(s3_copied, 1)
                    act.dma_start(beta_dram, beta_sb).then_inc(beta_stored, DMA)
                if pos == 2:
                    act.dma_start(ident[:, :], ident_in).then_inc(ident_landed, DMA)
                    act.dma_start(flip, flip_in).then_inc(ident_landed, DMA)
                    act.dma_start(masks_wide, masks_in).then_inc(const_landed, DMA)
                    act.dma_start(hg_gain[:, :], hg_gain_in).then_inc(const_landed, DMA)
                if pos == 7:
                    act.wait_ge(beta_stored, DMA)
                    act.dma_start(bias_rev, bass.AP(tensor=beta_dram.tensor, offset=beta_dram.offset,
                                                    ap=[[1, P], [BETA, HEADS], [1, SEQ]])).then_inc(bias_landed, DMA)
                if pos == 11:
                    for i in range(2):
                        act.wait_ge(flip_done, i + 1)
                        nc.scalar.activation(r4[:, i * 512:(i + 1) * 512], small[i][:, :], ACT.Copy).then_inc(bias_ready, 1)
                if pos == 13:
                    rstd(s1[:, 0:TT], rstd_x, NORM_X)
                    act.wait_ge(rstd_ready, NORM_X)
                    copy_out(JOB_G, acc[0][0][:, :], proj_a[:, 0, :], rstd_x[:, 0:1], 0)
            rstd(s2[:, 0:TT], rstd_m, NORM_MEM)
            act.wait_ge(rstd_ready, NORM_MEM)
            act.wait_ge(const_landed, 2 * DMA)

            with act.Fori(0, HEADS - 1) as h:
                for pos in range(BODY_G):
                    split_hi(G_BODY + pos, 2 * (NT if pos < 2 * JOB_G else NB), h, BODY_G)
                    head_steps(pos, h, h * BODY_G + G_BODY)
                    if pos == 2 * JOB_G + 2:
                        copy_out(h * BODY_G + (G_BODY + 2 * JOB_G), acc[0][0][:, :], proj_a[:, 0, :], rstd_x[:, 0:1], 0)

            q_cq, q_ffn = G_CQ - G_LAST_HEAD, G_FFN - G_LAST_HEAD
            for q in range(q_ffn + 10):
                for k, start, n0 in ((0, q_cq, 0), (1, q_ffn, 8)):
                    if q == start + 3:
                        square_sub(n0 + 3, 3, G_LAST_HEAD + start, k)
                        rstd(ssq, rstd_n, NORM_OUT + 2 * k)
                        operand_hi(k, 0)
                        operand_hi(k, 1)
                split_hi(G_LAST_HEAD + q)
                head_steps(q, HEADS - 1, G_LAST_HEAD)
                if q in (5, 6):
                    c0 = 7 * (q - 5)
                    act.wait_ge(s3_copied, HEADS)
                    nc.scalar.activation(a_hi[:, c0:c0 + 7, :], mix_t[:, c0:c0 + 7, :], ACT.Copy).then_inc(a_hi_ready, 1)
                if q == 11:
                    act.wait_ge(attn_copied, HEADS)
                    nc.scalar.activation(a_hi[:, 14, :], mix_t[:, 14, :], ACT.Copy).then_inc(a_hi_ready, 1)
                if q == 17:
                    act.wait_ge(s3_copied, HEADS + 1)
                    nc.scalar.activation(a_hi[:, 15, :], mix_t[:, 15, :], ACT.Copy).then_inc(a_hi_ready, 1)
                for k, start, n0 in ((0, q_cq, 0), (1, q_ffn, 8)):
                    for m in range(3):
                        if q == start - (3 - m) * JOB_G + 2:
                            square_sub(n0 + m, m, G_LAST_HEAD + start - (3 - m) * JOB_G, k)
                    next_operand(q - start, k)
                for j in range(CROSS_HEADS):
                    cross_steps(q - q_cq - (j + 1) * JOB_G, j, G_CQ + (j + 1) * JOB_G)
            nc.scalar.preload_act_table(ACT.Silu)

            for i, (tile0, tiles, g0, n0) in enumerate(groups):
                for pos in range(10 if i == 0 else 0, 2 * JOB_G):
                    split_hi(g0 + pos)
                    if i and pos == 2:
                        act_down(i - 1, 3, g0)
                    if pos == 10:
                        silu_gate(g0 + JOB_G)
                with act.Fori(0, tiles - 1) as f:
                    for pos in range(2 * JOB_G):
                        split_hi(g0 + 2 * JOB_G + pos, 2 * NT, f, 2 * JOB_G)
                        if pos == 4:
                            hidden_hi(f + tile0, f)
                        if pos == 10:
                            silu_gate(f * (2 * JOB_G) + (g0 + 3 * JOB_G))
                if i == 2:
                    nc.scalar.preload_act_table_set("natural_log_exp_and_others")
                per_job = tiles * F_CHUNKS // 2
                g1, n1 = g0 + tiles * 2 * JOB_G, n0 + 2 * tiles
                for pos in range(4 * per_job):
                    split_hi(g1 + pos)
                    if pos == 4:
                        hidden_hi(tile0 + tiles - 1, tiles - 1)
                    for m in range(3):
                        if pos == (m + 1) * per_job + 2:
                            act_down(i, m, g1 + (m + 1) * per_job)
            act_down(2, 3, 0)
            rstd(ssq, rstd_n, NORM_Y)
            act.wait_ge(rstd_ready, NORM_Y)
            act.wait_ge(yg_ready, 8)
            for n, t in OUT_POOL:
                cols = slice(n * NT, (n + 1) * NT)
                nc.scalar.activation(yg[:, t, cols], yg[:, t, cols], ACT.Copy,
                                     scale=rstd_n[:, t:t + 1]).then_inc(y_scaled, 1)

        @block.vector
        def _(dve):
            def split_lo(g, width=2 * NT, it=0, per=0):
                slot = g % RING
                dve.wait_ge(hi_ready, it * per + (g + 1))
                nc.vector.tensor_tensor(w_lo[:, slot, 0:width], raw[:, slot, 0:width],
                                        w_hi[:, slot, 0:width].bitcast(F32), ALU.subtract).then_inc(lo_ready, 1)

            def copy_out(used, bank, to, scale, pair):
                dve.wait_ge(granule_used, used)
                nc.vector.tensor_scalar(to, bank, scale, None, ALU.mult).then_inc(acc_free[pair], 1)

            def masked_pairs(l, bank, col):
                return (att.rearrange("p (t n) -> p t n", t=TT), masks[:, l, :].unsqueeze(1).to_broadcast((P, TT, P)),
                        bank[:, col:col + SEQ].rearrange("p (t n) -> p t n", t=TT))

            def merge(h, k, l, bank, col):
                dve.wait_ge(level_done, h * 8 + (k // 2 * 2 + 2))
                dve.wait_ge(level_merged, h * 8 + k)
                dve.nop(nofuse=True)
                nc.vector.copy_predicated(*masked_pairs(l, bank, col)).then_inc(level_merged, 1)

            def factors(l):
                m = 1 << l
                halves = decay[:, l, :].rearrange("p (n x m) -> p n x m", x=2, m=m)
                k_halves = kk.rearrange("p (n x m) -> p n x m", x=2, m=m)
                q_halves = qg.rearrange("p (n x m) -> p n x m", x=2, m=m)
                nc.vector.tensor_tensor(halves[:, :, 0, :], halves[:, :, 0, :], k_halves[:, :, 0, :], ALU.mult)
                nc.vector.tensor_tensor(halves[:, :, 1, :], halves[:, :, 1, :], q_halves[:, :, 1, :],
                                        ALU.mult).then_inc(factors_ready, 1)

            def head_steps(pos, h, used):
                if pos == 2:
                    copy_out(used, acc[1][1][:, 0:NB], proj_b[:, 1, :], rstd_x[:, 1:2], 1)
                if pos == 4:
                    dve.wait_ge(sig_ready, h + 1)
                    nc.vector.tensor_scalar(kk, sig[:, 0:SEQ], -1.0, 1.0, ALU.mult, ALU.add).then_inc(kk_ready, 1)
                    nc.vector.tensor_tensor(qg, s1[:, SEQ:2 * SEQ], sig[:, SEQ:2 * SEQ], ALU.mult).then_inc(qg_ready, 1)
                if pos == 5:
                    dve.wait_ge(logf_ready, h + 1)
                    for t in range(TT):
                        ts = slice(t * P, (t + 1) * P)
                        scan = nc.vector.tensor_tensor_scan(b[:, ts], ones[:, :], logf[:, ts], 0.0, ALU.mult, ALU.add)
                    scan.then_inc(b_ready, 1)
                    dve.wait_ge(scores_done, h + 1)
                    bias_h = bias[:, h, :]
                    nc.vector.scalar_tensor_tensor(prob[:, 0:SEQ], s2[:, 0:SEQ], DH ** -0.5, bias_h,
                                                   ALU.mult, ALU.add)
                    nc.vector.scalar_tensor_tensor(prob[:, SEQ:SEQ + P], s2[:, SEQ:SEQ + P], DH ** -0.5,
                                                   bias[:, h, P:SEQ], ALU.mult, ALU.add).then_inc(logits_ready, 1)
                    dve.wait_ge(logits_ready, h + 1)
                    nc.vector.tensor_reduce(neg_max[:, 1:2], prob[:, 0:SEQ], AX.X, ALU.max,
                                            negate=True).then_inc(max_ready, 1)
                    nc.vector.tensor_reduce(neg_max[:, 0:1], prob[:, SEQ:SEQ + P], AX.X, ALU.max,
                                            negate=True).then_inc(max_ready, 1)
                if pos == 7:
                    dve.wait_ge(prob_exp, h + 1)
                    nc.vector.reciprocal(row_sum, row_sum).then_inc(sum_inv, 1)
                    dve.wait_ge(sum_inv, h + 1)
                    nc.vector.tensor_scalar(prob[:, 0:SEQ], prob[:, 0:SEQ], row_sum[:, 1:2], None,
                                            ALU.mult).then_inc(prob_ready, 1)
                    nc.vector.tensor_scalar(prob[:, SEQ:SEQ + P], prob[:, SEQ:SEQ + P], row_sum[:, 0:1], None,
                                            ALU.mult).then_inc(prob_ready, 1)
                if pos == 8:
                    dve.wait_ge(gz_sig, h + 1)
                    nc.vector.tensor_tensor(gsil, gsil, proj_b[:, :, 2 * DH:3 * DH], ALU.mult).then_inc(gz_silu, 1)
                if pos == 9:
                    dve.wait_ge(decay_ready, h * 2 + 1)
                    for l in range(4):
                        factors(l)
                if pos == 10:
                    copy_out(used + JOB_G, acc[0][1][:, :], ckv[:, 1, bass.ds(h * NT, NT)], rstd_m[:, 1:2], 0)
                    dve.wait_ge(decay_ready, h * 2 + 2)
                    for l in range(4, 7):
                        factors(l)
                    nc.vector.tensor_tensor(decay[:, LEVELS, 0:P], decay[:, LEVELS, 0:P], kk[:, 0:P], ALU.mult)
                    nc.vector.tensor_tensor(decay[:, LEVELS, P:SEQ], decay[:, LEVELS, P:SEQ], qg[:, P:SEQ],
                                            ALU.mult).then_inc(factors_ready, 1)
                if pos == 11:
                    dve.wait_ge(level_done, h * 8 + 2)
                    nc.vector.tensor_tensor(att.rearrange("p (t n) -> p t n", t=TT),
                                            s0[:, 0:SEQ].rearrange("p (t n) -> p t n", t=TT),
                                            ident[:, :].unsqueeze(1).to_broadcast((P, TT, P)),
                                            ALU.mult).then_inc(level_merged, 1)
                    merge(h, 1, 0, s0, SEQ)
                if pos == 12:
                    merge(h, 2, 1, s1, 0)
                    merge(h, 3, 2, s1, SEQ)
                    merge(h, 4, 3, s3, 0)
                if pos == 13:
                    merge(h, 5, 4, s3, SEQ)
                    merge(h, 6, 5, s0, 0)
                    merge(h, 7, 6, s0, SEQ)
                if pos == 15:
                    dve.wait_ge(o_rstd, h + 1)
                    for t in range(TT):
                        y = nc.vector.scalar_tensor_tensor(y_hg[:, t, :], s2[:, t * DH:(t + 1) * DH],
                                                           rstd_o[:, t:t + 1], gsil[:, t, :], ALU.mult, ALU.mult)
                    y.then_inc(y_ready, 1)

            def gain_sub(n, m, used, k):
                pair = tail_pair(n)
                dve.wait_ge(gain_landed, (k + 1) * DMA)
                dve.wait_ge(granule_used, used)
                cols = slice(m * NT, (m + 1) * NT)
                nc.vector.tensor_tensor(sub[:, 0, cols], acc[pair][0][:, :], gain_row[:, cols],
                                        ALU.mult).then_inc(sub0_scaled, 1)
                dve.wait_ge(sub1_squared, 4 * k + m + 1)
                nc.vector.tensor_tensor(sub[:, 1, cols], acc[pair][1][:, :], gain_row[:, cols],
                                        ALU.mult).then_inc(acc_free[pair], 1)

            def residual(k, n):
                for t in range(TT):
                    cols = slice(n * NT, (n + 1) * NT)
                    nc.vector.scalar_tensor_tensor(res[:, t, cols], sub[:, t, cols], rstd_n[:, t:t + 1],
                                                   res[:, t, cols], ALU.mult, ALU.add).then_inc(res_ready, 1)

            def operand_lo(k, n):
                for chunk in range(4 * n, 4 * n + 4):
                    i, c = (chunk - 4 * n) // 2, chunk % 2
                    dve.wait_ge(a_hi_ready, A_PIECES + DC * k + (chunk | 1) + 1)
                    nc.vector.scalar_tensor_tensor(a_lo[:, chunk, :],
                                                   small[(2 * n + i) % 4][:, c * SEQ:(c + 1) * SEQ],
                                                   gcol[:, 2 + k, chunk:chunk + 1],
                                                   a_hi[:, chunk, :].bitcast(F32),
                                                   ALU.mult, ALU.subtract).then_inc(a_lo_ready, 1)

            def first_residual(k, n3):
                for n in (n3 - 1, n3):
                    dve.wait_ge(acc_free[tail_pair(n)], 2 * tail_uses(n) + 2)
                nc.vector.tensor_reduce(ssq, ssq_n, AX.X, ALU.add).then_inc(squares_ready, 1)
                if k == 0:
                    dve.wait_ge(res_landed, DMA)
                dve.wait_ge(rstd_ready, NORM_OUT + 2 * k)
                residual(k, 0)
                residual(k, 1)
                operand_lo(k, 0)
                operand_lo(k, 1)

            def next_operand(pos, k):
                if pos in (3, 4):
                    residual(k, pos - 1)
                for n in (2, 3):
                    if pos == TURN_AT[n] + 3:
                        operand_lo(k, n)
                if pos == 9:
                    dve.wait_ge(res_squared, 8 * k + 8)
                    nc.vector.tensor_reduce(ssq, ssq_r, AX.X, ALU.add).then_inc(squares_ready, 1)
                    dve.wait_ge(rstd_ready, NORM_CQ + 2 * k)

            def cross_steps(pos, j, used):
                if pos == 2:
                    n = 4 + j
                    copy_out(used, acc[tail_pair(n)][1][:, :], cq[:, 1, :], rstd_r[:, 1:2], tail_pair(n))
                if pos == 3:
                    dve.wait_ge(cqk_turned, 4 * j + 2)
                    nc.vector.tensor_copy(cq_t[:, 2:4, :], s1[:, :].rearrange("p (c s) -> p c s", c=2)).then_inc(cqk_t_ready, 1)
                    dve.wait_ge(cqk_turned, 4 * j + 4)
                    nc.vector.tensor_copy(ck_t[:, 2:4, :], s3[:, :].rearrange("p (c s) -> p c s", c=2)).then_inc(cqk_t_ready, 1)
                if pos == 5:
                    dve.wait_ge(cscores_done, j + 1)
                    nc.vector.tensor_reduce(neg_max, s0[:, :].rearrange("p (t m) -> p t m", t=TT), AX.X, ALU.max,
                                            negate=True).then_inc(cmax_ready, 1)
                    dve.wait_ge(cmax_ready, j + 1)
                    nc.vector.tensor_scalar(neg_max, neg_max, CROSS_DH ** -0.5, None, ALU.mult).then_inc(cbias_ready, 1)
                    dve.wait_ge(cprob_exp, j + 1)
                    nc.vector.reciprocal(row_sum, row_sum).then_inc(csum_inv, 1)
                    dve.wait_ge(csum_inv, j + 1)
                    for t in range(TT):
                        p = nc.vector.tensor_scalar(cprob[:, t, :], cprob[:, t, :], row_sum[:, t:t + 1], None, ALU.mult)
                    p.then_inc(cprob_ready, 1)
                if pos == 8:
                    for i in range(2):
                        dve.wait_ge(b_hi_ready, DC + 2 * j + i + 1)
                        pair = slice(4 * j + 2 * i, 4 * j + 2 * i + 2)
                        nc.vector.tensor_tensor(b_lo[:, pair, :], small[2 + i][:, :].rearrange("p (c s) -> p c s", c=2),
                                                b_hi[:, pair, :].bitcast(F32), ALU.subtract).then_inc(b_lo_ready, 1)

            def hidden(used, gate_uses):
                dve.wait_ge(granule_used, used)
                dve.wait_ge(acc_free[1], gate_uses * 2 + 2)
                for t in range(TT):
                    nc.vector.scalar_tensor_tensor(hid[:, t, :], acc[0][t][:, :], rstd_r[:, t:t + 1], gs[:, t, :],
                                                   ALU.mult, ALU.mult).then_inc(acc_free[0], 1)

            def hidden_lo(tile, ft):
                for i in range(2):
                    dve.wait_ge(b_hi_ready, tile * 2 + (DC + 8 + i + 1))
                    pair = bass.ds(ft * F_CHUNKS + 2 * i, 2)
                    nc.vector.tensor_tensor(b_lo[:, pair, :], small[i][:, :].rearrange("p (c s) -> p c s", c=2),
                                            b_hi[:, pair, :].bitcast(F32), ALU.subtract).then_inc(b_lo_ready, 1)

            def down(i, m, used):
                n = groups[i][3] + 2 * groups[i][1] + m
                pair, cols = tail_pair(n), slice(m * NT, (m + 1) * NT)
                dve.wait_ge(granule_used, used)
                if i == 0:
                    nc.vector.tensor_copy(sub[:, 1, cols], acc[pair][1][:, :]).then_inc(acc_free[pair], 1)
                    return
                before = groups[i - 1][3] + 2 * groups[i - 1][1] + m
                dve.wait_ge(acc_free[tail_pair(before)], 2 * tail_uses(before) + 2)
                for t in range(TT):
                    nc.vector.tensor_tensor(sub[:, t, cols], acc[pair][t][:, :], sub[:, t, cols],
                                            ALU.add).then_inc(acc_free[pair], 1)
                if i == 2:
                    dve.wait_ge(gain_landed, 3 * DMA)
                    dve.wait_ge(acc_free[pair], 2 * tail_uses(n) + 2)
                    for t in range(TT):
                        if m == 3 and t == 1:
                            dve.wait_ge(y_squared, 4)
                            nc.vector.tensor_reduce(ssq, ssq_n, AX.X, ALU.add).then_inc(squares_ready, 1)
                        nc.vector.tensor_tensor(yg[:, t, cols], sub[:, t, cols], gain_row[:, cols],
                                                ALU.mult).then_inc(yg_ready, 1)

            dve.wait_ge(gcol_landed, DMA)
            for pos in range(G_BODY):
                j = pos % JOB_G
                source, hi, lo, hi_count, lo_count, norm = (
                    (x_t, a_hi, a_lo, a_hi_ready, a_lo_ready, 0) if pos < JOB_G else
                    (mem_t, b_hi, b_lo, b_hi_ready, b_lo_ready, 1))
                for c in (2 * j, 2 * j + 1):
                    dve.wait_ge(hi_count, c + 1)
                    nc.vector.scalar_tensor_tensor(lo[:, c, :], source[:, c, :], gcol[:, norm, c:c + 1],
                                                   hi[:, c, :].bitcast(F32), ALU.mult, ALU.subtract).then_inc(lo_count, 1)
                split_lo(pos, 2 * (NT if pos < JOB_G else NB))
                if pos == 11:
                    for i in range(2, 4):
                        dve.wait_ge(flip_done, i + 1)
                        nc.vector.tensor_copy(r4[:, i * 512:(i + 1) * 512], small[i][:, :]).then_inc(bias_ready, 1)
                if pos == 13:
                    dve.wait_ge(rstd_ready, NORM_X)
                    copy_out(JOB_G, acc[0][1][:, :], proj_a[:, 1, :], rstd_x[:, 1:2], 0)
            dve.wait_ge(const_landed, 2 * DMA)
            nc.vector.tensor_copy(masks[:, :, :], masks_wide).then_inc(masks_ready, 1)
            dve.wait_ge(masks_ready, 1)
            dve.wait_ge(ident_landed, 2 * DMA)
            dve.wait_ge(bias_ready, 4)
            dve.wait_ge(consts_set, 1)
            dve.wait_ge(rstd_ready, NORM_MEM)

            with dve.Fori(0, HEADS - 1) as h:
                for pos in range(BODY_G):
                    split_lo(G_BODY + pos, 2 * (NT if pos < 2 * JOB_G else NB), h, BODY_G)
                    head_steps(pos, h, h * BODY_G + G_BODY)
                    if pos == 2 * JOB_G + 2:
                        copy_out(h * BODY_G + (G_BODY + 2 * JOB_G), acc[0][1][:, :], proj_a[:, 1, :], rstd_x[:, 1:2], 0)

            q_cq, q_ffn = G_CQ - G_LAST_HEAD, G_FFN - G_LAST_HEAD
            for q in range(q_ffn + 10):
                for k, start, n0 in ((0, q_cq, 0), (1, q_ffn, 8)):
                    if q == start + 3:
                        gain_sub(n0 + 3, 3, G_LAST_HEAD + start, k)
                        first_residual(k, n0 + 3)
                split_lo(G_LAST_HEAD + q)
                head_steps(q, HEADS - 1, G_LAST_HEAD)
                for at, chunks in ((6, slice(0, 7)), (7, slice(7, 14)), (12, slice(14, 15)), (17, slice(15, 16))):
                    if q == at:
                        dve.wait_ge(a_hi_ready, DC + 1 + (6, 7, 12, 17).index(at))
                        nc.vector.tensor_tensor(a_lo[:, chunks, :], mix_t[:, chunks, :], a_hi[:, chunks, :].bitcast(F32),
                                                ALU.subtract).then_inc(a_lo_ready, 1)
                for k, start, n0 in ((0, q_cq, 0), (1, q_ffn, 8)):
                    for m in range(3):
                        if q == start - (3 - m) * JOB_G + 2:
                            gain_sub(n0 + m, m, G_LAST_HEAD + start - (3 - m) * JOB_G, k)
                    next_operand(q - start, k)
                for j in range(CROSS_HEADS):
                    cross_steps(q - q_cq - (j + 1) * JOB_G, j, G_CQ + (j + 1) * JOB_G)

            for i, (tile0, tiles, g0, n0) in enumerate(groups):
                for pos in range(10 if i == 0 else 0, 2 * JOB_G):
                    split_lo(g0 + pos)
                    if i and pos == 2:
                        down(i - 1, 3, g0)
                with dve.Fori(0, tiles - 1) as f:
                    for pos in range(2 * JOB_G):
                        split_lo(g0 + 2 * JOB_G + pos, 2 * NT, f, 2 * JOB_G)
                        if pos == 2:
                            hidden(f * (2 * JOB_G) + (g0 + 2 * JOB_G), f + tail_uses(n0))
                        if pos == 5:
                            hidden_lo(f + tile0, f)
                per_job = tiles * F_CHUNKS // 2
                g1, n1 = g0 + tiles * 2 * JOB_G, n0 + 2 * tiles
                for pos in range(4 * per_job):
                    split_lo(g1 + pos)
                    if pos == 2:
                        hidden(g1, tail_uses(n1 - 2))
                    if pos == 5:
                        hidden_lo(tile0 + tiles - 1, tiles - 1)
                    for m in range(3):
                        if pos == (m + 1) * per_job + 2:
                            down(i, m, g1 + (m + 1) * per_job)
            down(2, 3, G_END)
            dve.wait_ge(rstd_ready, NORM_Y)
            dve.wait_ge(yg_ready, 8)
            for n, t in OUT_VECTOR:
                cols = slice(n * NT, (n + 1) * NT)
                nc.vector.scalar_tensor_tensor(res[:, t, cols], yg[:, t, cols], rstd_n[:, t:t + 1],
                                               res[:, t, cols], ALU.mult, ALU.add).then_inc(out_ready, 1)

        @block.gpsimd
        def _(pool):
            nc.gpsimd.memset(rel_sb[REL_BUCKETS:REL_BUCKETS + 1, :], 1.0).then_inc(rel_ones_set, 1)
            pool.wait_ge(rel_ones_set, 1)
            nc.gpsimd.memset(ones[:, :], 1.0)
            nc.gpsimd.memset(eps_col, EPS).then_inc(consts_set, 1)
            for j in range(JOB_G):
                pool.wait_ge(xt_landed[j], DMA)
                pair = x_t[:, 2 * j:2 * j + 2, :].rearrange("p c s -> p (c s)")
                if j == 0:
                    nc.gpsimd.tensor_tensor(x_sum, pair, pair, ALU.mult).then_inc(x_summed, 1)
                    continue
                pool.wait_ge(x_summed, j)
                nc.gpsimd.tensor_tensor(x_squares, pair, pair, ALU.mult).then_inc(x_squared, 1)
                pool.wait_ge(x_squared, j)
                nc.gpsimd.tensor_tensor(x_sum, x_sum, x_squares, ALU.add).then_inc(x_summed, 1)
            for j in range(1, JOB_G):
                pool.wait_ge(mem_squared, j + 1)
                if j > 1:
                    pool.wait_ge(mem_summed, j - 1)
                nc.gpsimd.tensor_tensor(mem_sum, mem_sum, mem_squares[:, j % 4, :], ALU.add).then_inc(mem_summed, 1)
            with pool.Fori(0, HEADS) as h:
                pool.wait_ge(b_ready, h + 1)
                for l in range(LEVELS):
                    m = 1 << l
                    halves = decay[:, l, :].rearrange("p (n x m) -> p n x m", x=2, m=m)
                    b_halves = b.rearrange("p (n x m) -> p n x m", x=2, m=m)
                    ref = b_halves[:, :, 0, m - 1:m].to_broadcast((P, SEQ // (2 * m), m))
                    nc.gpsimd.tensor_tensor(halves[:, :, 0, :], ref, b_halves[:, :, 0, :], ALU.subtract)
                    nc.gpsimd.tensor_tensor(halves[:, :, 1, :], b_halves[:, :, 1, :], ref,
                                            ALU.subtract).then_inc(decay_log, 1)
                nc.gpsimd.tensor_tensor(decay[:, LEVELS, 0:P], b[:, P - 1:P].to_broadcast((P, P)), b[:, 0:P],
                                        ALU.subtract)
                nc.gpsimd.tensor_copy(decay[:, LEVELS, P:SEQ], b[:, P:SEQ]).then_inc(decay_log, 1)
            for i, (n, t) in enumerate(OUT_POOL):
                cols = slice(n * NT, (n + 1) * NT)
                pool.wait_ge(y_scaled, i + 1)
                nc.gpsimd.tensor_tensor(res[:, t, cols], yg[:, t, cols], res[:, t, cols],
                                        ALU.add).then_inc(out_ready_pool, 1)


def _granules(w, width):
    rows, cols = w.shape
    return np.ascontiguousarray(w.reshape(rows // (2 * P), 2, P, cols // width, width).transpose(3, 0, 2, 1, 4)
                                ).reshape(cols // width, rows // (2 * P), P, 2 * width)


def _distance_table():
    exact = REL_BUCKETS // 2
    table = np.zeros((REL_BUCKETS + 1, BETA), np.float32)
    for i in range(BETA):
        d = SEQ - 1 - i
        count = sum(d % dilation == 0 and d <= window for window, dilation in BRANCHES) if d >= 0 else 0
        if d >= 0:
            bucket = d if d < exact else min(REL_BUCKETS - 1, exact + int(
                np.float32(math.log(d / exact) / math.log(REL_MAX_DIST / exact) * (REL_BUCKETS - exact))))
            table[bucket, i] = 1.0
        table[REL_BUCKETS, i] = math.log(count) if count else MASKED
    return table


def _level_masks():
    s, t = np.arange(P)[:, None], np.arange(P)[None, :]
    return np.stack([((s >> (l + 1)) == (t >> (l + 1))) & ((s >> l) % 2 == 0) & ((t >> l) % 2 == 1)
                     for l in range(LEVELS)], axis=1).astype(np.int32)


def kernel(x, mem, rel_bias, lb_logits, norm_gains, w_in, hg_norm, w_out, w_cq, w_ckv, w_co, w_gate_up, w_down):
    import concourse.bacc as bacc
    from concourse.bass_utils import run_bass_kernel_spmd

    a = {k: np.asarray(v) for k, v in dict(
        x=x, mem=mem, rel_bias=rel_bias, gains=norm_gains, w_in=w_in, hg_norm=hg_norm, w_out=w_out, w_cq=w_cq,
        w_ckv=w_ckv, w_co=w_co, w_gate_up=w_gate_up, w_down=w_down).items()}
    gains = a["gains"][0]
    by_head = a["w_in"][0].reshape(D, 7, HEADS, DH)
    in_a = by_head[:, 0:4].transpose(0, 2, 1, 3).reshape(D, HEADS * NT)
    in_b = by_head[:, 4:7].transpose(0, 2, 1, 3).reshape(D, HEADS * NB)
    mix_order = [*range(7), *range(8, 15), 7, 15]
    out_w = a["w_out"][0].reshape(DC, P, D)[mix_order].reshape(D, D)
    gate, up = _granules(a["w_gate_up"][0][:, :D_FF], NT), _granules(a["w_gate_up"][0][:, D_FF:], NT)
    cols = lambda g: g.reshape(DC, P).T
    arrays = {
        "x": a["x"][0],
        "xt": np.ascontiguousarray(a["x"][0].T),
        "memt": np.ascontiguousarray(a["mem"][0].T),
        "rel_bias": a["rel_bias"],
        "ident": np.eye(P, dtype=np.float32),
        "flip": np.ascontiguousarray(np.eye(P, dtype=np.float32)[::-1]),
        "masks": _level_masks(),
        "onehot": _distance_table(),
        "gain_cols": np.ascontiguousarray(np.stack([cols(gains[i]) for i in (0, 3, 2, 5)], axis=1)),
        "gain_rows": np.ascontiguousarray(gains[[1, 4, 6]]),
        "hg_gain": np.ascontiguousarray(a["hg_norm"][0].reshape(HEADS, DH).T),
        "w_in_a": _granules(in_a, NT),
        "w_in_b": _granules(in_b, NB),
        "w_ckv": _granules(a["w_ckv"][0], NT),
        "w_out": _granules(out_w, NT),
        "w_cq": _granules(a["w_cq"][0], NT),
        "w_co": _granules(a["w_co"][0], NT),
        "w_gate_up": np.ascontiguousarray(np.stack([gate, up], axis=1)),
        "w_down": _granules(a["w_down"][0], NT),
    }
    nc = bacc.Bacc("TRN2", target_bir_lowering=False, num_devices=1)
    args, maps = [], {}
    for name, value in arrays.items():
        maps[f"in_{name}"] = value
        args.append(nc.dram_tensor(f"in_{name}", value.shape, mybir.dt.from_np(value.dtype), kind="ExternalInput").ap())
    beta = nc.dram_tensor("beta", (HEADS, BETA), F32, kind="Internal").ap()
    out = nc.dram_tensor("out_0", (SEQ, D), F32, kind="ExternalOutput").ap()
    layer_kernel(nc, *args, beta, out)
    result = run_bass_kernel_spmd(nc, [maps], core_ids=[0])
    return result.results[0]["out_0"].reshape(1, SEQ, D)
```
